# Optimizing a Trainium2 kernel written in Bass

```python
import jax, jax.numpy as jnp
from jax import lax
import numpy as np

D_MODEL = 1024
BATCH = 1
SEQ = 512
DEPTH = 2

D_MIX = 1024
DA_HEADS = 4
DA_HEAD_DIM = 64
DA_V_DIM = 2 * DA_HEAD_DIM
DA_QK = DA_HEADS * 2 * DA_HEAD_DIM
DA_WIDTH = DA_HEADS * DA_V_DIM
HG_HEADS = 4
HG_K_DIM = 128
HG_V_DIM = 128
HG_K = HG_HEADS * HG_K_DIM
HG_WIDTH = HG_HEADS * HG_V_DIM
IN_SIZES = (DA_QK, DA_QK, DA_WIDTH, HG_K, HG_K, HG_K, HG_WIDTH, HG_WIDTH)
D_IN = DA_QK * 2 + DA_WIDTH + HG_K * 3 + HG_WIDTH * 2
D_FF = 2816
CONV_WIDTH = 3
ROPE_THETA = 10000.0
Q_BLOCK = 128
CHUNK = 64
EPS = 1e-6
EXP_CLAMP = 30.0

kernel_name = "hybrid_diffattn_hgrn2_convglu_encoder"

def rms_norm(x, g):
    xf = x.astype(jnp.float32)
    y = xf * lax.rsqrt(jnp.mean(xf * xf, axis=-1, keepdims=True) + EPS)
    return (y * g.astype(jnp.float32)).astype(x.dtype)

def rope_tables(positions):
    half = DA_HEAD_DIM // 2
    inv_freq = ROPE_THETA ** (-jnp.arange(half, dtype=jnp.float32) / half)
    ang = positions.astype(jnp.float32)[:, None, None, :, None] * inv_freq
    return jnp.cos(ang), jnp.sin(ang)

def apply_rope(t, cos, sin):
    tf = t.astype(jnp.float32)
    t1, t2 = jnp.split(tf, 2, axis=-1)
    return jnp.concatenate([t1 * cos - t2 * sin, t2 * cos + t1 * sin], axis=-1).astype(t.dtype)

def split_cols(p, sizes):
    idx = []
    acc = 0
    for s in sizes[:-1]:
        acc += s
        idx.append(acc)
    return jnp.split(p, idx, axis=-1)

def to_heads(t, n_heads):
    b, s, _ = t.shape
    return t.reshape(b, s, n_heads, -1).transpose(0, 2, 1, 3)

def diff_attention(q, k, v, cos, sin, q_g, k_g, lam, lam_init, out_g):
    b, s, _ = q.shape
    q = rms_norm(q.reshape(b, s, DA_HEADS, 2, DA_HEAD_DIM), q_g)
    k = rms_norm(k.reshape(b, s, DA_HEADS, 2, DA_HEAD_DIM), k_g)
    q = apply_rope(q.transpose(0, 2, 3, 1, 4), cos, sin) * (DA_HEAD_DIM ** -0.5)
    k = apply_rope(k.transpose(0, 2, 3, 1, 4), cos, sin)
    v = to_heads(v, DA_HEADS)
    n_blocks = s // Q_BLOCK
    qb = jnp.moveaxis(q.reshape(b, DA_HEADS, 2, n_blocks, Q_BLOCK, DA_HEAD_DIM), 3, 0)

    def block(qi):
        scores = jnp.einsum('bhcqd,bhckd->bhcqk', qi, k).astype(jnp.float32)
        probs = jax.nn.softmax(scores, axis=-1)
        weights = probs[:, :, 0] - lam * probs[:, :, 1]
        return jnp.einsum('bhqk,bhkv->bhqv', weights.astype(v.dtype), v)

    o = lax.map(block, qb)
    o = o.transpose(1, 0, 3, 2, 4).reshape(b, s, DA_HEADS, DA_V_DIM)
    o = rms_norm(o, out_g) * (1.0 - lam_init)
    return o.reshape(b, s, DA_WIDTH)

def gla_chunk_scan(q, k, v, log_f):
    b, h, s, dk = q.shape
    dv = v.shape[-1]
    n = s // CHUNK

    def chunks(t):
        return jnp.moveaxis(t.reshape(b, h, n, CHUNK, t.shape[-1]), 2, 0)

    qc, kc, vc = chunks(q), chunks(k), chunks(v)
    bc = jnp.cumsum(chunks(log_f), axis=-2)
    mask = jnp.tril(jnp.ones((CHUNK, CHUNK), dtype=bool))[:, :, None]

    def step(state, inp):
        q_, k_, v_, b_ = inp
        diff = b_[:, :, :, None, :] - b_[:, :, None, :, :]
        decay = jnp.where(mask, jnp.exp(jnp.where(mask, diff, 0.0)), 0.0)
        scores = jnp.einsum('bhtd,bhsd,bhtsd->bhts', q_, k_, decay)
        b_last = b_[:, :, -1:, :]
        o = (jnp.einsum('bhts,bhsv->bhtv', scores, v_)
             + jnp.einsum('bhtd,bhdv->bhtv', q_ * jnp.exp(b_), state))
        state = (jnp.exp(b_last)[:, :, 0, :, None] * state
                 + jnp.einsum('bhsd,bhsv->bhdv', k_ * jnp.exp(b_last - b_), v_))
        return state, o

    state0 = jnp.zeros((b, h, dk, dv), jnp.float32)
    _, o = lax.scan(step, state0, (qc, kc, vc, bc))
    return jnp.moveaxis(o, 0, 2).reshape(b, h, s, dv)

def hgrn2_bidirectional(q, z_fwd, z_bwd, inp, gate, lb_fwd, lb_bwd, out_g):
    b, s, _ = q.shape
    qh = to_heads(q, HG_HEADS).astype(jnp.float32)
    ih = to_heads(inp, HG_HEADS).astype(jnp.float32)

    def gates(z, lb):
        zh = to_heads(z, HG_HEADS).astype(jnp.float32)
        lbh = lb.astype(jnp.float32).reshape(HG_HEADS, 1, HG_K_DIM)
        log_f = jax.nn.log_sigmoid(zh) + jnp.log1p(lbh * jnp.exp(jnp.minimum(-zh, EXP_CLAMP)))
        log_f = jnp.minimum(log_f, 0.0)
        key = (1.0 - lbh) * jax.nn.sigmoid(-zh)
        return key, log_f

    k_f, lf_f = gates(z_fwd, lb_fwd)
    k_b, lf_b = gates(z_bwd, lb_bwd)
    o_fwd = gla_chunk_scan(qh, k_f, ih, lf_f)
    flip = lambda t: jnp.flip(t, axis=2)
    o_bwd = flip(gla_chunk_scan(flip(qh), flip(k_b), flip(ih), flip(lf_b)))
    o = (o_fwd + o_bwd).transpose(0, 2, 1, 3).astype(q.dtype)
    g = gate.reshape(b, s, HG_HEADS, HG_V_DIM)
    o = rms_norm(o, out_g) * jax.nn.silu(g)
    return o.reshape(b, s, HG_WIDTH)

def conv_glu_ffn(h, w_up, conv_w, conv_b, w_down):
    u = h @ w_up
    up = jnp.pad(u, ((0, 0), (1, 1), (0, 0)))
    u = conv_w[0] * up[:, :-2] + conv_w[1] * up[:, 1:-1] + conv_w[2] * up[:, 2:] + conv_b
    a, v = jnp.split(u, 2, axis=-1)
    return (jax.nn.silu(a) * v) @ w_down

def setup_inputs(seed: int = 0) -> dict:
    key = jax.random.key(seed)
    ks = jax.random.split(key, 24)
    f32 = jnp.float32
    nrm = lambda k, shape, scale: jax.random.normal(k, shape, f32) * scale
    gain = lambda k, shape: 1.0 + 0.02 * jax.random.normal(k, shape, f32)
    x = jax.random.normal(ks[0], (BATCH, SEQ, D_MODEL), f32)
    offsets = jax.random.randint(ks[1], (BATCH, 1), 0, 1024, dtype=jnp.int32)
    positions = (jnp.arange(SEQ, dtype=jnp.int32)[None, :] + offsets).astype(jnp.int32)
    return {
        "x": x,
        "positions": positions,
        "mix_norm_g": gain(ks[2], (DEPTH, D_MODEL)),
        "w_in": nrm(ks[3], (DEPTH, D_MODEL, D_IN), D_MODEL ** -0.5),
        "q_norm_g": gain(ks[4], (DEPTH, DA_HEAD_DIM)),
        "k_norm_g": gain(ks[5], (DEPTH, DA_HEAD_DIM)),
        "lam_q1": nrm(ks[6], (DEPTH, DA_HEAD_DIM), 0.1),
        "lam_k1": nrm(ks[7], (DEPTH, DA_HEAD_DIM), 0.1),
        "lam_q2": nrm(ks[8], (DEPTH, DA_HEAD_DIM), 0.1),
        "lam_k2": nrm(ks[9], (DEPTH, DA_HEAD_DIM), 0.1),
        "diff_out_g": gain(ks[10], (DEPTH, DA_V_DIM)),
        "hg_lb_logits": nrm(ks[11], (DEPTH, 2, HG_K), 0.5),
        "hg_out_g": gain(ks[12], (DEPTH, HG_V_DIM)),
        "w_out": nrm(ks[13], (DEPTH, D_MIX, D_MODEL), D_MIX ** -0.5),
        "ffn_norm_g": gain(ks[14], (DEPTH, D_MODEL)),
        "w_up": nrm(ks[15], (DEPTH, D_MODEL, 2 * D_FF), D_MODEL ** -0.5),
        "conv_w": nrm(ks[16], (DEPTH, CONV_WIDTH, 2 * D_FF), CONV_WIDTH ** -0.5),
        "conv_b": nrm(ks[17], (DEPTH, 2 * D_FF), 0.02),
        "w_down": nrm(ks[18], (DEPTH, D_FF, D_MODEL), D_FF ** -0.5),
    }

def reference(x, positions, mix_norm_g, w_in, q_norm_g, k_norm_g, lam_q1, lam_k1, lam_q2, lam_k2,
              diff_out_g, hg_lb_logits, hg_out_g, w_out, ffn_norm_g, w_up, conv_w, conv_b, w_down):
    cos, sin = rope_tables(positions)
    p = jax.nn.softmax(hg_lb_logits.astype(jnp.float32), axis=0)
    lower_bounds = jnp.clip(jnp.cumsum(p, axis=0) - p[0:1], 0.0, 1.0 - 1e-4)
    for l in range(DEPTH):
        h = rms_norm(x, mix_norm_g[l])
        proj = h @ w_in[l]
        da_q, da_k, da_v, hg_q, hg_zf, hg_zb, hg_i, hg_g = split_cols(proj, IN_SIZES)
        lam_init = 0.8 - 0.6 * float(np.exp(-0.3 * l))
        lam = (jnp.exp(jnp.sum(lam_q1[l].astype(jnp.float32) * lam_k1[l].astype(jnp.float32)))
               - jnp.exp(jnp.sum(lam_q2[l].astype(jnp.float32) * lam_k2[l].astype(jnp.float32)))
               + lam_init)
        y_a = diff_attention(da_q, da_k, da_v, cos, sin, q_norm_g[l], k_norm_g[l], lam, lam_init, diff_out_g[l])
        y_b = hgrn2_bidirectional(hg_q, hg_zf, hg_zb, hg_i, hg_g,
                                  lower_bounds[l, 0], lower_bounds[l, 1], hg_out_g[l])
        x = x + jnp.concatenate([y_a, y_b.astype(y_a.dtype)], axis=-1) @ w_out[l]
        x = x + conv_glu_ffn(rms_norm(x, ffn_norm_g[l]), w_up[l], conv_w[l], conv_b[l], w_down[l])
    return x


_drawn_inputs = setup_inputs


def setup_inputs(seed=0):
    import zlib

    import numpy as np

    out = dict(_drawn_inputs(seed))
    spreads = {}
    factors = {'q_norm_g': 4.876,
     'k_norm_g': 4.176,
     'lam_q2': 5.402,
     'diff_out_g': 3.582,
     'hg_out_g': 5.563,
     'ffn_norm_g': 2.987,
     'conv_b': 3.035}
    for name, (base, spread) in spreads.items():
        noise = np.random.default_rng([zlib.crc32(name.encode()), seed]).standard_normal(out[name].shape)
        drawn = base * np.exp(spread * noise) if base else spread * noise
        out[name] = __import__('jax').numpy.asarray(drawn.astype(out[name].dtype))
    for name, factor in factors.items():
        out[name] = (out[name] * factor).astype(out[name].dtype)
    return out
```

```python
from contextlib import ExitStack

import numpy as np
import concourse.bass as bass
from concourse import mybir

F32 = mybir.dt.float32
F32R = mybir.dt.float32r
I32 = mybir.dt.int32
U32 = mybir.dt.uint32
ALU = mybir.AluOpType
ACT = mybir.ActivationFunctionType
AX = mybir.AxisListType

P = 128
D = 1024
S = 512
DEPTH = 2
HEADS = 4
HD = 64
DFF = 2816
EPS = 1e-6
KT = D // P
TT = S // P
FT = DFF // P

UNIT = KT * P
N_IN, N_OUT, N_UP, N_DOWN = 32, 8, 2 * FT, FT
U_OUT = N_IN
U_UP = U_OUT + N_OUT
U_DOWN = U_UP + N_UP
UNITS = U_DOWN + N_DOWN
U_ZF, U_ZB, U_HQ, U_HI, U_DQ, U_DK, U_HG, U_DV = range(0, 32, 4)

LEVELS = 11

C_IDENT = 0
C_MASK = P
C_MEAN_D = C_MASK + 7 * P
C_MEAN_V = C_MEAN_D + P
C_MEAN_H = C_MEAN_V + P
C_ONE = C_MEAN_H + P
C_ROT = C_ONE + P
C_FREQ = C_ROT + P
C_LAM = C_FREQ + 1
C_OML = C_LAM + DEPTH
C_EPS = C_OML + DEPTH
C_LN8 = C_EPS + 1
NC = C_LN8 + 1

R_MIXG, R_FFNG, R_QG, R_KG, R_DAG, R_HGG = 0, 8, 16, 17, 18, 19
R_LAM = 20
R_CONV = 24
NR = R_CONV + 8 * (FT + 2)


class Chain:

    def __init__(self, eng, sem, base=0):
        self.eng, self.sem, self.base, self.n = eng, sem, base, 0

    def __call__(self, ins):
        ins.then_inc(self.sem, 1)
        self.n += 1
        self.eng.wait_ge(self.sem, self.base + self.n)


def build(nc, xT, wts, cst, par, lbl, pos, outT):
    ctx = ExitStack()
    mix = ExitStack()
    ffn = ExitStack()

    def sb(name, shape, dt=F32, scope=ctx):
        return scope.enter_context(nc.sbuf_tensor(name, shape, dt))

    def sem(name):
        s = ctx.enter_context(nc.semaphore(name))
        layer_sems.append(s)
        return s

    layer_sems = []
    with ctx:
        x = sb("x", [P, KT, S])
        hH = sb("hH", [P, KT, S], F32R)
        hL = sb("hL", [P, KT, S], F32R)
        raw = sb("raw", [P, 2, UNIT])
        wH = sb("wH", [P, 2, UNIT], F32R)
        wL = sb("wL", [P, 2, UNIT], F32R)
        C = sb("C", [P, NC])
        R = sb("R", [P, NR])
        cosT = sb("cosT", [P, S])
        sinT = sb("sinT", [P, S])
        sq = sb("sq", [P, 2, S])
        lnv = sb("lnv", [P, S])
        rstd = sb("rstd", [P, 2, S])
        tmp = sb("tmp", [P, 2, S])
        rotg = sb("rotg", [P, 2, P])
        lball = sb("lball", [P, DEPTH, 8])
        lb = sb("lb", [P, 8])
        omlb = sb("omlb", [P, 8])
        lamc = sb("lamc", [P, 8])
        dag = sb("dag", [P, 1])
        sm = sb("sm", [P, 16, 8])
        cw = sb("cw", [P, 2, 8])
        bank = [ctx.enter_context(nc.psum_tensor(f"bank{i}", [P, S], F32)) for i in range(8)]

        KK = sb("KK", [P, 2, HEADS * S], F32, mix)
        QQ = sb("QQ", [P, 2, HEADS * S], F32, mix)
        T = sb("T", [P, 2, HEADS * S], F32, mix)
        A = sb("A", [P, HEADS, TT, S], F32, mix)
        HI = sb("HI", [P, TT, S], F32, mix)
        QK = sb("QK", [P, 8, S], F32, mix)
        sig = sb("sig", [P, 2, S], F32, mix)
        mix.close()
        gH = sb("gH", [P, FT * S], F32R, ffn)
        gL = sb("gL", [P, FT * S], F32R, ffn)
        ua = sb("ua", [P, 2, S], F32, ffn)
        uv = sb("uv", [P, 2, S], F32, ffn)
        gt = sb("gt", [P, 2, S], F32, ffn)
        ffn.close()
        Af = A[:].rearrange("p h s t -> p (h s t)")
        sp = Af[:, 0:2 * S].rearrange("p (b t) -> p b t", b=2)
        sn = Af[:, 2 * S:4 * S].rearrange("p (b t) -> p b t", b=2)
        tt = Af[:, 4 * S:5 * S]
        ksum = QK[:, 4:8, :].rearrange("p a t -> p (a t)")
        tot2 = ksum.rearrange("p (d n) -> p d n", d=2)
        V = KK[:, 0, :].rearrange("p (s c) -> p s c", s=TT)
        oh = QQ[:, 0, :].rearrange("p (h t) -> p h t", h=HEADS)
        E = Af[:, 0:4 * S].rearrange("p (b c t) -> p b c t", b=2, c=2)
        wT = Af[:, 4 * S:12 * S].rearrange("p (b k q) -> p b k q", b=2, k=TT)

        par_in = sem("par_in")
        raw_in = [sem("raw_in0"), sem("raw_in1")]
        w_high = sem("w_high")
        w_split = sem("w_split")
        w_used = sem("w_used")
        gate_w = sem("gate_w")
        set_up = sem("set_up")
        lam_sum = sem("lam_sum")
        lam_exp = sem("lam_exp")
        lam_done = sem("lam_done")
        x_upd = sem("x_upd")
        sq_ready = sem("sq_ready")
        sq_used = sem("sq_used")
        ln_done = sem("ln_done")
        rstd_ready = sem("rstd_ready")
        hn_ready = sem("hn_ready")
        hH_ready = sem("hH_ready")
        h_ready = sem("h_ready")
        acc_free = sem("acc_free")
        z_done = sem("z_done")
        tm_ev = sem("tm_ev")
        hg_ready = sem("hg_ready")
        lv_mm = sem("lv_mm")
        a_cp = sem("a_cp")
        a_msk = sem("a_msk")
        av_mm = sem("av_mm")
        o_ev = sem("o_ev")
        qk_aux = sem("qk_aux")
        qk_ln = sem("qk_ln")
        qk_rstd = sem("qk_rstd")
        rope_r = sem("rope_r")
        rope_done = sem("rope_done")
        gs_done = sem("gs_done")
        sc_mm = sem("sc_mm")
        neg_max = sem("neg_max")
        exps = sem("exps")
        w_ready = sem("w_ready")
        tr_mm = sem("tr_mm")
        wT_ready = sem("wT_ready")
        pv_mm = sem("pv_mm")
        o_sq = sem("o_sq")
        o_sum = sem("o_sum")
        o_ln = sem("o_ln")
        o_rstd = sem("o_rstd")
        y_ready = sem("y_ready")
        yH_ready = sem("yH_ready")
        yL_ready = sem("yL_ready")
        wo_done = sem("wo_done")
        conv_init = sem("conv_init")
        conv_done = sem("conv_done")
        silu_done = sem("silu_done")
        g_ready = sem("g_ready")
        gH_ready = sem("gH_ready")
        gL_ready = sem("gL_ready")
        gate_a = sem("gate_a")
        wd_done = sem("wd_done")
        dve_own = sem("dve_own")
        dve_ffn = sem("dve_ffn")
        pre_in = ctx.enter_context(nc.semaphore("pre_in"))
        pre_dve = ctx.enter_context(nc.semaphore("pre_dve"))
        pre_act = ctx.enter_context(nc.semaphore("pre_act"))
        out_done = ctx.enter_context(nc.semaphore("out_done"))

        def gs(hd):
            return T[:, hd // 2, 1024 + hd % 2 * S:1024 + (hd % 2 + 1) * S]

        def cst_at(c, n=P):
            return C[:, c:c + n]

        def blocks(v, h):
            return v.rearrange("p (n two h) -> p n two h", two=2, h=h)

        def diag(hd):
            v = A[:]
            return bass.AP(tensor=v.tensor, offset=hd * TT * S, ap=[[HEADS * TT * S, P], [S + P, TT], [1, P]])

        posi = T[:, 0, 0:S].bitcast(I32)
        ang, kk, kh, m0 = T[:, 0, S:2 * S], T[:, 1, 0:S], T[:, 1, S:2 * S], T[:, 1, 2 * S:3 * S]
        lraw, le, lp = sm[:, 0:2, :], sm[:, 2:4, :], sm[:, 4:6, :]
        lmax, lsum = sm[:, 6, :], sm[:, 7, :]
        with nc.Block() as block:
            @block.sync
            def _(sp_):
                sp_.dma_start(C[:], cst).then_inc(pre_in, 16)
                sp_.dma_start(posi, pos).then_inc(pre_in, 16)
                sp_.dma_start(lraw, lbl).then_inc(pre_in, 16)
                sp_.dma_start(x[:], xT).then_inc(pre_in, 16)
                sp_.wait_ge(pre_in, 64)

            @block.vector
            def _(dve):
                ch = Chain(dve, pre_dve)
                TWO_PI = 2 * np.pi
                c1 = float(np.floor(TWO_PI * 2 ** 9) / 2 ** 9)
                c2 = float(np.floor((TWO_PI - c1) * 2 ** 21) / 2 ** 21)
                c3 = float(np.float32(TWO_PI - c1 - c2))
                BIG = float(1.5 * 2 ** 23)
                PI = float(np.nextafter(np.float32(np.pi), np.float32(0)))
                dve.wait_ge(pre_in, 64)
                ch(dve.tensor_copy(kk, posi))
                ch(dve.tensor_scalar(ang, kk, C[:, C_FREQ:C_FREQ + 1], None, ALU.mult))
                ch(dve.tensor_scalar(kk, ang, float(1 / TWO_PI), BIG, ALU.mult, ALU.add))
                ch(dve.tensor_scalar(kk, kk, -BIG, None, ALU.add))
                ch(dve.tensor_scalar(kh, kk, 1 / 2048, BIG, ALU.mult, ALU.add))
                ch(dve.tensor_scalar(kh, kh, -BIG, 2048.0, ALU.add, ALU.mult))
                ch(dve.tensor_tensor(kk, kk, kh, ALU.subtract))
                for c in (c1, c2, c3):
                    ch(dve.scalar_tensor_tensor(ang, kh, -c, ang, ALU.mult, ALU.add))
                    ch(dve.scalar_tensor_tensor(ang, kk, -c, ang, ALU.mult, ALU.add))
                ch(dve.tensor_scalar(kk, ang, float(np.pi / 2), None, ALU.add))
                ch(dve.tensor_scalar(m0, kk, float(np.pi), -TWO_PI, ALU.is_gt, ALU.mult))
                ch(dve.tensor_tensor(kk, kk, m0, ALU.add))
                ch(dve.tensor_scalar(kk, kk, PI, -PI, ALU.min, ALU.max))
                ch(dve.tensor_scalar(ang, ang, PI, -PI, ALU.min, ALU.max))
                ch(dve.tensor_copy(lmax, lraw[:, 0, :]))
                for l in range(1, DEPTH):
                    ch(dve.tensor_tensor(lmax, lmax, lraw[:, l, :], ALU.max))
                for l in range(DEPTH):
                    ch(dve.tensor_tensor(le[:, l, :], lraw[:, l, :], lmax, ALU.subtract))
                dve.wait_ge(pre_act, 3)
                ch(dve.tensor_copy(lsum, le[:, 0, :]))
                for l in range(1, DEPTH):
                    ch(dve.tensor_tensor(lsum, lsum, le[:, l, :], ALU.add))
                ch(dve.reciprocal(lsum, lsum))
                for l in range(DEPTH):
                    ch(dve.tensor_tensor(lp[:, l, :], le[:, l, :], lsum, ALU.mult))
                ch(dve.tensor_copy(lmax, lp[:, 0, :]))
                for l in range(DEPTH):
                    if l:
                        ch(dve.tensor_tensor(lmax, lmax, lp[:, l, :], ALU.add))
                    ch(dve.tensor_tensor(lball[:, l, :], lmax, lp[:, 0, :], ALU.subtract))
                    ch(dve.tensor_scalar(lball[:, l, :], lball[:, l, :], 0.0, 1.0 - 1e-4, ALU.max, ALU.min))

            @block.scalar
            def _(act):
                act.wait_ge(pre_dve, 20 + DEPTH)
                act.activation(le, le, ACT.Exp).then_inc(pre_act, 1)
                act.activation(cosT[:], kk, ACT.Sin).then_inc(pre_act, 1)
                act.activation(sinT[:], ang, ACT.Sin).then_inc(pre_act, 1)

        with nc.Fori(0, DEPTH) as layer:
            with nc.Block() as block:
                @block.sync
                def _(sp_):
                    sp_.dma_start(R[:], par[bass.ds(layer, 1)].rearrange("a p n -> (a p) n")).then_inc(par_in, 16)

                    def load(s, row):
                        sp_.dma_start(raw[:, s, :], wts[bass.ds(row, 1)].rearrange("a p n -> (a p) n"))\
                           .then_inc(raw_in[s], 16)

                    for s in range(2):
                        load(s, layer * UNITS + s)
                    with sp_.Fori(1, UNITS // 2) as j:
                        for s in range(2):
                            row = layer * UNITS + j * 2 + s
                            sp_.wait_ge(w_split, j * 2 + s - 1)
                            load(s, row)

                @block.gpsimd
                def _(pool):
                    def split(j, s, first):
                        pool.wait_ge(raw_in[s], j * 16 + 16)
                        if not first:
                            pool.wait_ge(w_used, j * 2 + s - 1)
                        pool.sem_inc(gate_w, 1)
                        pool.tensor_scalar(wH[:, s, :], raw[:, s, :], 1.0, 1.0, ALU.mult, ALU.mult).then_inc(w_high, 1)
                        pool.wait_ge(w_high, j * 2 + s + 1)
                        pool.tensor_tensor(wL[:, s, :], raw[:, s, :], wH[:, s, :].bitcast(F32), ALU.subtract)\
                            .then_inc(w_split, 1)

                    for s in range(2):
                        split(0, s, True)
                    with pool.Fori(1, UNITS // 2) as j:
                        for s in range(2):
                            split(j, s, False)

                @block.tensor
                def _(pe):
                    def triple(out, s, wcols, rhs_h, rhs_l, first, last):
                        a, b = wcols
                        pe.matmul(out, wH[:, s, a:b], rhs_h, start=first, stop=False)
                        pe.matmul(out, wL[:, s, a:b], rhs_h, start=False, stop=False)
                        return pe.matmul(out, wH[:, s, a:b], rhs_l, start=False, stop=last)

                    def sums(n):
                        for k in range(KT):
                            pe.wait_ge(sq_ready, 8 * n + k + 1)
                            pe.matmul(bank[0][:], cst_at(C_MEAN_D), sq[:, k % 2, :], start=k == 0, stop=k == KT - 1)\
                                .then_inc(sq_used, 1)

                    def column(u, out, h_base=None):
                        s = u % 2
                        pe.wait_ge(w_split, u + 1)
                        for k in range(KT):
                            if h_base is not None:
                                pe.wait_ge(h_ready, h_base + k + 1)
                            m = triple(out, s, (k * P, k * P + P), hH[:, k, :], hL[:, k, :], k == 0, k == KT - 1)
                        m.then_inc(w_used, 1)

                    def rows(u):
                        s, kb = u % 2, 2 * (u % 4)
                        pe.wait_ge(w_split, u + 1)
                        for i in range(TT):
                            if kb == 0:
                                if u > U_HI:
                                    pe.wait_ge(o_ev, i + 1)
                            for k2 in range(2):
                                k, w = kb + k2, slice(k2 * S, k2 * S + S)
                                t = slice(i * P, i * P + P)
                                first, last = k == 0, k == KT - 1
                                pe.matmul(bank[2 + i][:], hH[:, k, t], wH[:, s, w], start=first, stop=False)
                                pe.matmul(bank[2 + i][:], hL[:, k, t], wH[:, s, w], start=False, stop=False)
                                m = pe.matmul(bank[2 + i][:], hH[:, k, t], wL[:, s, w], start=False, stop=last)
                        m.then_inc(w_used, 1)

                    def level(lv):
                        pe.wait_ge(hg_ready, min(lv, 9) + 1)
                        for hd in range(HEADS):
                            b = bank[2 + hd]
                            if lv == 0:
                                pe.wait_ge(tm_ev, 4)
                            elif lv == 1 or lv > 8:
                                pe.wait_ge(a_cp, (0 if lv == 1 else 4 * (lv - 8)) + hd + 1)
                            else:
                                pe.wait_ge(a_msk, 4 * (lv - 2) + hd + 1)
                            col = lambda t, plane, i, n=1: t[:, plane, hd * S + i * P:hd * S + (i + n) * P]
                            if lv <= 8:
                                for i in range(TT):
                                    o = b[:, i * P:i * P + P]
                                    if lv == 0:
                                        m = pe.matmul(o, ksum[:, hd * S + i * P:hd * S + i * P + P], col(QQ, 1, i),
                                                      start=True, stop=True)
                                    elif lv < 8:
                                        h = 2 ** (lv - 1)
                                        for d in range(2):
                                            m = pe.matmul(blocks(o, h)[:, :, 1 - d, :], col(KK, d, i),
                                                          blocks(col(QQ, 1 - d, i), h)[:, :, 1 - d, :],
                                                          start=True, stop=True)
                                    else:
                                        m = pe.matmul(o, col(KK, i % 2, i), col(QQ, 1 - i % 2, i ^ 1),
                                                      start=True, stop=True)
                            else:
                                half = lv - 9
                                for i in range(2):
                                    m = pe.matmul(b[:, i * 2 * P:(i + 1) * 2 * P], col(KK, half, 2 * half + i),
                                                  col(QQ, 1 - half, 2 - 2 * half, 2), start=True, stop=True)
                            m.then_inc(lv_mm, 1)

                    def aux(n):
                        pe.wait_ge(acc_free, 12 + n + 1)
                        if n:
                            pe.wait_ge(qk_ln, n)
                            pe.wait_ge(rope_r, n)
                        pe.matmul(bank[6][:], cst_at(C_MEAN_H), sq[:, n % 2, :], start=True, stop=True)
                        pe.matmul(bank[7][:], rotg[:, n // 4, :], QK[:, n, :], start=True, stop=True).then_inc(qk_aux, 1)

                    def feature(u, f):
                        if f >= 2:
                            pe.wait_ge(acc_free, f - 1)
                        column(u, bank[f % 2][:], 0 if u == 0 else None)

                    pe.wait_ge(set_up, 1)
                    pe.matmul(bank[1][:, 0:2], cst_at(C_ONE), lamc[:, 0:2], start=True, stop=True).then_inc(lam_sum, 1)
                    sums(0)
                    pe.wait_ge(ln_done, 1)
                    pe.wait_ge(lam_exp, 1)
                    for u in range(U_HI):
                        feature(u, u)
                    for u in range(U_HI, U_HI + 4):
                        rows(u)
                    for g, u in enumerate(range(U_DQ, U_DQ + 12)):
                        feature(u, 12 + g)
                        if 1 <= g <= 8:
                            aux(g - 1)
                        if g < LEVELS:
                            level(g)
                    for hd in range(HEADS):
                        pe.wait_ge(a_cp, 12 + hd + 1)
                        for i in range(TT):
                            m = pe.matmul(bank[2 + hd][:], HI[:, i, hd * P:hd * P + P], A[:, hd, i, :],
                                          start=i == 0, stop=i == TT - 1)
                        m.then_inc(av_mm, 1)
                    for u in range(U_DV, U_DV + 4):
                        rows(u)

                    def scores(a):
                        hd, qt = divmod(a, 4)
                        if a == 0:
                            pe.wait_ge(acc_free, 24)
                            pe.wait_ge(rope_done, 8)
                        if a == 1:
                            pe.wait_ge(tm_ev, 8)
                        if a >= 2:
                            pe.wait_ge(exps, a - 1)
                        for c in range(2):
                            r = slice(HD * c, HD * c + HD)
                            m = pe.matmul(bank[2 * (a % 2) + c][:], QK[r, hd, qt * P:qt * P + P], QK[r, 4 + hd, :],
                                          start=True, stop=True)
                        m.then_inc(sc_mm, 1)

                    def turn(a):
                        pe.wait_ge(w_ready, a + 1)
                        if a == 0:
                            pe.wait_ge(tm_ev, 8)
                        if a >= 2:
                            pe.wait_ge(wT_ready, a - 1)
                        for k in range(TT):
                            m = pe.transpose(bank[4 + a % 2][:, k * P:k * P + P], E[:, a % 2, 0, k * P:k * P + P],
                                             cst_at(C_IDENT))
                        m.then_inc(tr_mm, 1)

                    def values(hd):
                        pe.wait_ge(wT_ready, 4 * hd + 4)
                        if hd:
                            pe.wait_ge(y_ready, 4 + hd)
                        for k in range(TT):
                            m = pe.matmul(bank[6][:], V[:, k, hd * P:hd * P + P], wT[:, hd % 2, k, :],
                                          start=k == 0, stop=k == TT - 1)
                        m.then_inc(pv_mm, 1)

                    def head_sum(p):
                        pe.wait_ge(o_sq, p + 1)
                        if p:
                            pe.wait_ge(o_ln, p)
                        pe.matmul(bank[7][:], cst_at(C_MEAN_V), sq[:, p % 2, :], start=True, stop=True)\
                            .then_inc(o_sum, 1)

                    scores(0)
                    scores(1)
                    for a in range(16):
                        if a + 2 < 16:
                            scores(a + 2)
                        turn(a)
                        if a < 4:
                            head_sum(a)
                        if a % 4 == 0 and a:
                            values(a // 4 - 1)
                        if a % 4 == 1 and a > 1:
                            head_sum(4 + a // 4 - 1)
                    values(3)
                    head_sum(7)

                    for p in range(KT):
                        u = U_OUT + p
                        pe.wait_ge(w_split, u + 1)
                        pe.wait_ge(yL_ready, p + 1)
                        for m_ in range(KT):
                            if p == 0 and m_ == 6:
                                pe.wait_ge(y_ready, 8)
                            if p == 0 and m_ == 7:
                                pe.wait_ge(o_ln, 8)
                            m = triple(bank[m_][:], u % 2, (m_ * P, m_ * P + P), hH[:, p, :], hL[:, p, :],
                                       p == 0, p == KT - 1)
                            if p == KT - 1 and m_ < KT - 1:
                                m.then_inc(wo_done, 1)
                        m.then_inc(w_used, 1)

                    pe.wait_ge(x_upd, 8)
                    sums(1)
                    pe.wait_ge(ln_done, 2)

                    def pair(i, q, first):
                        for c in range(2):
                            s = c
                            pe.wait_ge(w_split, i * 4 + (U_UP + 2 * q + c + 1))
                            if not first:
                                pe.wait_ge(conv_done, i * 4 + (2 * (q - 2) + c + 1))
                            for k in range(KT):
                                if first and q == 0 and c == 0:
                                    pe.wait_ge(h_ready, 8 + k + 1)
                                m = triple(bank[2 * q + c][:], s, (k * P, k * P + P), hH[:, k, :], hL[:, k, :],
                                           k == 0, k == KT - 1)
                            m.then_inc(w_used, 1)

                    for q in range(2):
                        pair(0, q, True)
                    with pe.Fori(1, FT // 2) as i:
                        for q in range(2):
                            pair(i, q, False)

                    def down(k, s, gh, gl, first, last):
                        pe.wait_ge(w_split, k + (U_DOWN + 1))
                        pe.wait_ge(gL_ready, k + 1)
                        for m_ in range(KT):
                            if first and m_ == 0:
                                pe.wait_ge(conv_done, 2 * FT)
                            m = triple(bank[m_][:], s, (m_ * P, m_ * P + P), gh, gl, first, last)
                            if last and m_ < KT - 1:
                                m.then_inc(wd_done, 1)
                        m.then_inc(w_used, 1)

                    for k in range(2):
                        down(k, k, gH[:, k * S:(k + 1) * S], gL[:, k * S:(k + 1) * S], k == 0, False)
                    with pe.Fori(1, FT // 2 - 1) as i:
                        for s in range(2):
                            down(i * 2 + s, s, gH[:, bass.ds(i * (2 * S) + s * S, S)],
                                 gL[:, bass.ds(i * (2 * S) + s * S, S)], False, False)
                    for k in range(FT - 2, FT):
                        down(k, k % 2, gH[:, k * S:(k + 1) * S], gL[:, k * S:(k + 1) * S], False, k == FT - 1)

                @block.scalar
                def _(act):
                    eps = EPS

                    def squares(n):
                        for k in range(KT):
                            if n:
                                act.wait_ge(x_upd, k + 1)
                            if k >= 2:
                                act.wait_ge(sq_used, 8 * n + k - 1)
                            act.activation(sq[:, k % 2, :], x[:, k, :], ACT.Square).then_inc(sq_ready, 1)

                    def norm(n):
                        act.wait_ge(sq_used, 8 * n + 8)
                        act.activation(lnv[:], bank[0][:], ACT.Ln, bias=cst_at(C_EPS, 1)).then_inc(ln_done, 1)
                        act.wait_ge(ln_done, n + 1)
                        act.activation(rstd[:, 0, :], lnv[:], ACT.Exp, scale=-0.5).then_inc(rstd_ready, 1)
                        for k in range(KT):
                            act.wait_ge(hn_ready, 8 * n + k + 1)
                            act.activation(hH[:, k, :], tmp[:, k % 2, :], ACT.Copy).then_inc(hH_ready, 1)

                    def tile_done(u):
                        act.wait_ge(w_used, u + 1)

                    act.wait_ge(lam_sum, 1)
                    act.activation(lamc[:, 2:4], bank[1][:, 0:2], ACT.Exp, scale=0.5).then_inc(lam_exp, 1)
                    squares(0)
                    norm(0)
                    for f in range(8):
                        tile_done(f)
                        if f >= 2:
                            act.wait_ge(z_done, f - 1)
                        act.activation(sp[:, f % 2, :], bank[f % 2][:], ACT.Sigmoid)
                        act.activation(sn[:, f % 2, :], bank[f % 2][:], ACT.Sigmoid, scale=-1.0).then_inc(acc_free, 1)
                    for hd in range(HEADS):
                        f = 8 + hd
                        tile_done(f)
                        act.activation(QQ[:, 1, hd * S:hd * S + S], bank[f % 2][:], ACT.Copy).then_inc(acc_free, 1)
                    tile_done(U_HI + 3)
                    for i in range(TT):
                        act.activation(HI[:, i, :], bank[2 + i][:], ACT.Copy).then_inc(tm_ev, 1)

                    def level_copy(lv):
                        for hd in range(HEADS):
                            act.wait_ge(lv_mm, 4 * lv + hd + 1)
                            b = bank[2 + hd][:].rearrange("p (i t) -> p i t", i=TT)
                            Ah = A[:, hd, :, :].rearrange("p s (i t) -> p s i t", t=P)
                            if lv == 0:
                                act.activation(diag(hd), b, ACT.Copy).then_inc(a_cp, 1)
                            elif lv == 8:
                                base, row = hd * TT * S, HEADS * TT * S
                                for o in range(2):
                                    dst = bass.AP(tensor=A[:].tensor, offset=base + (P if o == 0 else S),
                                                  ap=[[row, P], [2 * S + 2 * P, 2], [1, P]])
                                    cp = act.activation(dst, b[:, o::2, :], ACT.Copy)
                                cp.then_inc(a_cp, 1)
                            else:
                                half = lv - 9
                                act.activation(A[:, hd, 2 * half:2 * half + 2, (2 - 2 * half) * P:(4 - 2 * half) * P],
                                               bank[2 + hd][:].rearrange("p (i t) -> p i t", i=2), ACT.Copy)\
                                    .then_inc(a_cp, 1)

                    def rope_stats(n):
                        act.wait_ge(qk_aux, n + 1)
                        if n:
                            act.wait_ge(qk_rstd, n)
                        act.activation(lnv[:], bank[6][:], ACT.Ln, bias=cst_at(C_EPS, 1)).then_inc(qk_ln, 1)
                        act.wait_ge(qk_ln, n + 1)
                        if n >= 2:
                            act.wait_ge(rope_done, n - 1)
                        act.activation(rstd[:, n % 2, :], lnv[:], ACT.Exp, scale=-0.5,
                                       bias=cst_at(C_LN8, 1) if n < 4 else 0.0).then_inc(qk_rstd, 1)

                    for g in range(12):
                        f = 12 + g
                        tile_done(U_DQ + g)
                        if g < 8:
                            if g >= 2:
                                act.wait_ge(qk_aux, g - 1)
                            if g == 4:
                                act.wait_ge(hg_ready, 5)
                            act.activation(QK[:, g, :], bank[f % 2][:], ACT.Copy)
                            act.activation(sq[:, g % 2, :], bank[f % 2][:], ACT.Square).then_inc(acc_free, 1)
                        else:
                            hd = g - 8
                            if hd >= 2:
                                act.wait_ge(gs_done, hd - 1)
                            act.activation(sig[:, hd % 2, :], bank[f % 2][:], ACT.Sigmoid)
                            act.activation(gs(hd), bank[f % 2][:], ACT.Copy).then_inc(acc_free, 1)
                        if 1 <= g <= 8:
                            rope_stats(g - 1)
                        if g == 0 or 8 <= g < LEVELS:
                            level_copy(g)
                    for hd in range(HEADS):
                        act.wait_ge(av_mm, hd + 1)
                        act.activation(oh[:, hd, :], bank[2 + hd][:], ACT.Copy).then_inc(o_ev, 1)
                    tile_done(U_DV + 3)
                    for i in range(TT):
                        act.activation(V[:, i, :], bank[2 + i][:], ACT.Copy).then_inc(tm_ev, 1)

                    def head_square(p):
                        if p < HEADS:
                            src = oh[:, p, :]
                            act.wait_ge(o_ev, p + 1)
                        else:
                            src = bank[6][:]
                            act.wait_ge(pv_mm, p - 3)
                        if p >= 2:
                            act.wait_ge(o_sum, p - 1)
                        act.activation(sq[:, p % 2, :], src, ACT.Square).then_inc(o_sq, 1)

                    def head_stats(p):
                        act.wait_ge(o_sum, p + 1)
                        if p:
                            act.wait_ge(o_rstd, p)
                        act.activation(lnv[:], bank[7][:], ACT.Ln, bias=cst_at(C_EPS, 1)).then_inc(o_ln, 1)
                        act.wait_ge(o_ln, p + 1)
                        if p >= 2:
                            act.wait_ge(y_ready, p - 1)
                        act.activation(rstd[:, p % 2, :], lnv[:], ACT.Exp, scale=-0.5).then_inc(o_rstd, 1)

                    def head_high(p):
                        act.wait_ge(y_ready, p + 1)
                        act.activation(hH[:, p, :], tmp[:, p % 2, :], ACT.Copy).then_inc(yH_ready, 1)

                    def back(a):
                        hd, qt = divmod(a, 4)
                        act.wait_ge(tr_mm, a + 1)
                        if hd >= 2:
                            act.wait_ge(pv_mm, hd - 1)
                        act.activation(wT[:, hd % 2, :, qt * P:qt * P + P],
                                       bank[4 + a % 2][:].rearrange("p (k q) -> p k q", k=TT), ACT.Copy)\
                            .then_inc(wT_ready, 1)

                    head_square(0)
                    for a in range(16):
                        act.wait_ge(neg_max, a + 1)
                        if a >= 2:
                            act.wait_ge(tr_mm, a - 1)
                        for c in range(2):
                            e = act.activation(E[:, a % 2, c, :], bank[2 * (a % 2) + c][:], ACT.Exp,
                                               bias=sm[:, a, c:c + 1], accum_out=sm[:, a, 2 + c:3 + c])
                        e.then_inc(exps, 1)
                        if a:
                            back(a - 1)
                        if 1 <= a <= 4:
                            head_stats(a - 1)
                            head_high(a - 1)
                            if a < 4:
                                head_square(a)
                        if a % 4 == 1 and a > 1:
                            head_square(4 + a // 4 - 1)
                        if a % 4 == 2 and a > 2:
                            head_stats(4 + a // 4 - 1)
                            head_high(4 + a // 4 - 1)
                    back(15)
                    head_square(7)
                    head_stats(7)
                    head_high(7)
                    squares(1)
                    norm(1)

                    def pair(i, q, first):
                        src = bank[2 * q], bank[2 * q + 1]
                        for c, dst in enumerate((ua, uv)):
                            if not first:
                                act.wait_ge(g_ready, i * 2 + (q - 1))
                            act.wait_ge(w_used, i * 4 + (U_UP + 2 * q + c + 1))
                            act.activation(dst[:, q, :], src[c][:], ACT.Identity, bias=cw[:, q, 4 * c + 3:4 * c + 4],
                                           scale=cw[:, q, 4 * c + 1:4 * c + 2]).then_inc(conv_init, 1)
                        act.wait_ge(conv_done, i * 4 + (2 * q + 1))
                        act.activation(ua[:, q, :], ua[:, q, :], ACT.Silu).then_inc(silu_done, 1)
                        act.wait_ge(g_ready, i * 2 + (q + 1))
                        act.sem_inc(gate_a, 1)
                        cols = gH[:, q * S:q * S + S] if first else gH[:, bass.ds(i * (2 * S) + q * S, S)]
                        act.activation(cols, gt[:, q, :], ACT.Copy).then_inc(gH_ready, 1)

                    for q in range(2):
                        pair(0, q, True)
                    with act.Fori(1, FT // 2) as i:
                        for q in range(2):
                            pair(i, q, False)

                @block.vector
                def _(dve):
                    ch = Chain(dve, dve_own)
                    dve.wait_ge(par_in, 16)
                    ch(dve.tensor_copy(lb[:], lball[:].rearrange("p l c -> p (l c)")[:, bass.ds(layer * 8, 8)]))
                    ch(dve.tensor_scalar(omlb[:], lb[:], -1.0, 1.0, ALU.mult, ALU.add))
                    ch(dve.tensor_copy(lamc[:, 4:5], C[:, bass.ds(layer + C_LAM, 1)]))
                    ch(dve.tensor_copy(lamc[:, 5:6], C[:, bass.ds(layer + C_OML, 1)]))
                    ch(dve.tensor_tensor(dag[:], R[:, R_DAG:R_DAG + 1], lamc[:, 5:6], ALU.mult))
                    for c in range(2):
                        ch(dve.tensor_scalar(rotg[:, c, :], cst_at(C_ROT), R[:, R_QG + c:R_QG + c + 1], None, ALU.mult))
                    lv4 = R[:, R_LAM:R_LAM + 4].rearrange("p (a b) -> p a b", b=2)
                    dve.tensor_tensor(lamc[:, 0:2], lv4[:, :, 0], lv4[:, :, 1], ALU.mult).then_inc(set_up, 1)
                    dve.wait_ge(lam_exp, 1)
                    ch(dve.tensor_tensor(lamc[:, 6:7], lamc[:, 3:4], lamc[:, 2:3], ALU.subtract))
                    ch(dve.tensor_tensor(lamc[:, 7:8], lamc[:, 6:7], lamc[:, 4:5], ALU.subtract))

                    def norm(n, col):
                        dve.wait_ge(rstd_ready, n + 1)

                        def low(k):
                            dve.wait_ge(hH_ready, 8 * n + k + 1)
                            dve.tensor_tensor(hL[:, k, :], tmp[:, k % 2, :], hH[:, k, :].bitcast(F32), ALU.subtract)\
                               .then_inc(h_ready, 1)

                        for k in range(KT):
                            if k >= 2:
                                dve.wait_ge(h_ready, 8 * n + k - 1)
                            dve.scalar_tensor_tensor(tmp[:, k % 2, :], x[:, k, :], R[:, col + k:col + k + 1],
                                                     rstd[:, 0, :], ALU.mult, ALU.mult).then_inc(hn_ready, 1)
                            if k:
                                low(k - 1)
                        low(KT - 1)

                    norm(0, R_MIXG)
                    e30 = float(np.exp(30.0))
                    for f in range(8):
                        d, hd = divmod(f, 4)
                        c = slice(hd * S, hd * S + S)
                        dve.wait_ge(acc_free, f + 1)
                        s_p, s_n = sp[:, f % 2, :], sn[:, f % 2, :]
                        ch(dve.tensor_scalar(tt, s_p, e30, 1.0, ALU.mult, ALU.min))
                        ch(dve.tensor_tensor(tt, tt, s_n, ALU.mult))
                        ch(dve.scalar_tensor_tensor(T[:, d, c], tt, lb[:, f:f + 1], s_p, ALU.mult, ALU.add))
                        ch(dve.tensor_scalar(T[:, d, c], T[:, d, c], 1.0, None, ALU.min))
                        dve.tensor_scalar(KK[:, d, c], s_n, omlb[:, f:f + 1], None, ALU.mult).then_inc(z_done, 1)
                    dve.wait_ge(z_done, 8)
                    dve.tensor_tensor(ksum, KK[:, 0, :], KK[:, 1, :], ALU.add).then_inc(hg_ready, 1)
                    dve.wait_ge(acc_free, 12)
                    ch(dve.tensor_tensor(QQ[:, 0, :], QQ[:, 1, :], T[:, 1, :], ALU.mult))

                    def grow(h, lv):
                        if h == 1:
                            tot = T
                        elif h == 2:
                            tot = tot2
                        else:
                            o = 1024 - 4096 // h
                            tot = T[:, :, o:o + 2048 // h]
                        n = HEADS * S // (2 * h)
                        for t, plane, half, d in ((QQ, 1, 1, 0), (KK, 0, 0, 0), (QQ, 0, 0, 1), (KK, 1, 1, 1)):
                            v = blocks(t[:, plane, :], h)[:, :, half, :]
                            w = tot[:, d, :].rearrange("p (n two) -> p n two", two=2)[:, :, 1 - half]
                            w = w.rearrange("p (n o) -> p n o", o=1).to_broadcast([P, n, h])
                            last = dve.tensor_tensor(v, v, w, ALU.mult)
                            if (t, plane) != (KK, 1):
                                last.then_inc(dve_own, 1)
                                ch.n += 1
                        last.then_inc(hg_ready, 1)
                        if h < 128:
                            nxt = tot2 if h == 1 else T[:, :, 1024 - 2048 // h:1024 - 2048 // h + 1024 // h]
                            for d in range(2):
                                w = tot[:, d, :].rearrange("p (n two) -> p n two", two=2)
                                dve.tensor_tensor(nxt[:, d, :], w[:, :, 0], w[:, :, 1], ALU.mult).then_inc(dve_own, 1)
                                ch.n += 1

                    def masked(lv):
                        m = C[:, C_MASK + (lv - 1) * P:C_MASK + lv * P].bitcast(U32)
                        m = m.rearrange("p (o t) -> p o t", o=1).to_broadcast([P, TT, P])
                        for hd in range(HEADS):
                            dve.wait_ge(lv_mm, 4 * lv + hd + 1)
                            if lv == 1:
                                dve.wait_ge(a_cp, hd + 1)
                            else:
                                dve.wait_ge(a_msk, 4 * (lv - 2) + hd + 1)
                            dve.copy_predicated(diag(hd), m, bank[2 + hd][:].rearrange("p (i t) -> p i t", i=TT))\
                               .then_inc(a_msk, 1)

                    def rope(n):
                        dve.wait_ge(acc_free, 12 + n + 1)
                        if n:
                            dve.wait_ge(rope_done, n)
                        ch(dve.scalar_tensor_tensor(tmp[:, 0, :], QK[:, n, :], R[:, R_QG + n // 4:R_QG + n // 4 + 1],
                                                    cosT[:], ALU.mult, ALU.mult))
                        dve.wait_ge(qk_aux, n + 1)
                        dve.tensor_tensor(tmp[:, 1, :], bank[7][:], sinT[:], ALU.mult).then_inc(rope_r, 1)
                        dve.wait_ge(rope_r, n + 1)
                        ch(dve.tensor_tensor(tmp[:, 0, :], tmp[:, 0, :], tmp[:, 1, :], ALU.add))
                        dve.wait_ge(qk_rstd, n + 1)
                        dve.tensor_tensor(QK[:, n, :], tmp[:, 0, :], rstd[:, n % 2, :], ALU.mult).then_inc(rope_done, 1)

                    for g in range(12):
                        if 1 <= g <= 8:
                            rope(g - 1)
                        if g == 0:
                            dve.wait_ge(lv_mm, 4)
                            dve.tensor_tensor(QQ[:, 1, :], QQ[:, 1, :], T[:, 0, :], ALU.mult).then_inc(hg_ready, 1)
                        if 1 <= g <= 8:
                            if g <= 7:
                                masked(g)
                            dve.wait_ge(lv_mm, 4 * g + 4)
                            dve.wait_ge(hg_ready, g + 1)
                            if ch.n:
                                dve.wait_ge(dve_own, ch.n)
                            grow(2 ** (g - 1), g)
                        if g >= 8:
                            hd = g - 8
                            dve.wait_ge(acc_free, 20 + hd + 1)
                            dve.tensor_tensor(gs(hd), gs(hd), sig[:, hd % 2, :], ALU.mult).then_inc(gs_done, 1)

                    def head_scale(p):
                        dve.wait_ge(o_rstd, p + 1)
                        if p >= 2:
                            dve.wait_ge(yL_ready, p - 1)
                        t = tmp[:, p % 2, :]
                        if p < HEADS:
                            ch(dve.scalar_tensor_tensor(t, oh[:, p, :], R[:, R_HGG:R_HGG + 1], rstd[:, p % 2, :],
                                                        ALU.mult, ALU.mult))
                            dve.tensor_tensor(t, t, gs(p), ALU.mult).then_inc(y_ready, 1)
                        else:
                            dve.scalar_tensor_tensor(t, bank[6][:], dag[:, 0:1], rstd[:, p % 2, :],
                                                     ALU.mult, ALU.mult).then_inc(y_ready, 1)

                    def head_low(p):
                        dve.wait_ge(yH_ready, p + 1)
                        dve.tensor_tensor(hL[:, p, :], tmp[:, p % 2, :], hH[:, p, :].bitcast(F32), ALU.subtract)\
                           .then_inc(yL_ready, 1)

                    def row_max(a):
                        dve.wait_ge(sc_mm, a + 1)
                        for c in range(2):
                            m = dve.tensor_reduce(sm[:, a, c:c + 1], bank[2 * (a % 2) + c][:], axis=AX.X, op=ALU.max,
                                                  negate=True)
                        m.then_inc(neg_max, 1)

                    def combine(a):
                        dve.wait_ge(exps, a + 1)
                        ch(dve.reciprocal(sm[:, a, 4:6], sm[:, a, 2:4]))
                        ch(dve.tensor_tensor(sm[:, a, 6:7], sm[:, a, 5:6], lamc[:, 7:8], ALU.mult))
                        ch(dve.tensor_scalar(E[:, a % 2, 0, :], E[:, a % 2, 0, :], sm[:, a, 4:5], None, ALU.mult))
                        dve.scalar_tensor_tensor(E[:, a % 2, 0, :], E[:, a % 2, 1, :], sm[:, a, 6:7],
                                                 E[:, a % 2, 0, :], ALU.mult, ALU.add).then_inc(w_ready, 1)

                    row_max(0)
                    for a in range(16):
                        if a + 1 < 16:
                            row_max(a + 1)
                        combine(a)
                        if 1 <= a <= 4:
                            head_scale(a - 1)
                            head_low(a - 1)
                        if a % 4 == 2 and a > 2:
                            head_scale(4 + a // 4 - 1)
                            head_low(4 + a // 4 - 1)
                    head_scale(7)
                    head_low(7)

                    for m_ in range(KT):
                        if m_ < KT - 1:
                            dve.wait_ge(wo_done, m_ + 1)
                        else:
                            dve.wait_ge(w_used, U_UP)
                        dve.tensor_tensor(x[:, m_, :], x[:, m_, :], bank[m_][:], ALU.add).then_inc(x_upd, 1)
                    for q in range(2):
                        ch(dve.tensor_copy(cw[:, q, :], R[:, R_CONV + 8 * q:R_CONV + 8 * q + 8]))
                    dve.wait_ge(x_upd, 8)
                    norm(1, R_FFNG)

                    STEPS = 8

                    def pair(i, q, first, own):
                        src = bank[2 * q], bank[2 * q + 1]
                        for c, dst in enumerate((ua, uv)):
                            w = lambda n: cw[:, q, 4 * c + n:4 * c + n + 1]
                            dve.wait_ge(conv_init, i * 4 + (2 * q + c + 1))
                            own(dve.scalar_tensor_tensor(dst[:, q, 1:S], src[c][:, 0:S - 1], w(0), dst[:, q, 1:S],
                                                         ALU.mult, ALU.add))
                            dve.scalar_tensor_tensor(dst[:, q, 0:S - 1], src[c][:, 1:S], w(2), dst[:, q, 0:S - 1],
                                                     ALU.mult, ALU.add).then_inc(conv_done, 1)
                        dve.wait_ge(silu_done, i * 2 + (q + 1))
                        dve.wait_ge(conv_done, i * 4 + (2 * q + 2))
                        dve.tensor_tensor(gt[:, q, :], ua[:, q, :], uv[:, q, :], ALU.mult).then_inc(g_ready, 1)
                        dve.wait_ge(gH_ready, i * 2 + (q + 1))
                        at = slice(q * S, q * S + S) if first else bass.ds(i * (2 * S) + q * S, S)
                        dve.tensor_tensor(gL[:, at], gt[:, q, :], gH[:, at].bitcast(F32), ALU.subtract)\
                           .then_inc(gL_ready, 1)
                        dve.wait_ge(gL_ready, i * 2 + (q + 1))
                        at = R_CONV + 8 * (q + 2)
                        nxt = R[:, at:at + 8] if first else R[:, bass.ds(i * 16 + at, 8)]
                        own(dve.tensor_copy(cw[:, q, :], nxt))

                    own = Chain(dve, dve_ffn)
                    for q in range(2):
                        pair(0, q, True, own)
                    per = own.n
                    with dve.Fori(1, FT // 2) as i:
                        own = Chain(dve, dve_ffn, i * per)
                        for q in range(2):
                            pair(i, q, False, own)
                    for m_ in range(KT):
                        if m_ < KT - 1:
                            dve.wait_ge(wd_done, m_ + 1)
                        else:
                            dve.wait_ge(w_used, UNITS)
                        dve.tensor_tensor(x[:, m_, :], x[:, m_, :], bank[m_][:], ALU.add).then_inc(x_upd, 1)

            with nc.Block() as block:
                @block.sync
                def _(sp_):
                    for s in layer_sems:
                        sp_.sem_clear(s)

        with nc.Block() as block:
            @block.sync
            def _(sp_):
                sp_.dma_start(outT, x[:]).then_inc(out_done, 16)
                sp_.wait_ge(out_done, 16)


def constants():
    c = np.zeros((P, NC), np.float32)
    i = np.arange(P)
    c[:, C_IDENT:C_IDENT + P] = np.eye(P)
    for n in range(7):
        h = 2 ** n
        b = i // h
        c[:, C_MASK + n * P:C_MASK + (n + 1) * P] = (b[:, None] ^ 1) == b[None, :]
    c[:, C_MEAN_D:C_MEAN_D + P] = 1 / D
    c[:, C_MEAN_V:C_MEAN_V + P] = 1 / P
    c[:, C_MEAN_H:C_MEAN_H + P] = (i[:, None] // HD == i[None, :] // HD) / HD
    c[:, C_ONE:C_ONE + P] = 1
    half = HD // 2
    for m in range(P):
        if m % HD < half:
            c[m + half, C_ROT + m] = -1
        else:
            c[m - half, C_ROT + m] = 1
    freq = np.float32(10000.0) ** (-np.arange(half, dtype=np.float32) / np.float32(half))
    c[:, C_FREQ] = freq[i % half]
    for l in range(DEPTH):
        lam_init = 0.8 - 0.6 * float(np.exp(-0.3 * l))
        c[:, C_LAM + l] = lam_init
        c[:, C_OML + l] = 1 - lam_init
    c[:, C_EPS] = EPS
    c[:, C_LN8] = -0.5 * np.log(HD)
    return c


def columns(w):
    d, r, n = w.shape
    return w.reshape(d, KT, P, n // P, P).transpose(0, 3, 2, 1, 4).reshape(d, n // P, P, KT * P)


def two_rows(w):
    d = w.shape[0]
    return w.reshape(d, 4, 2, P, S).transpose(0, 1, 3, 2, 4).reshape(d, 4, P, 2 * S)


def kernel(**inputs):
    import concourse.bacc as bacc
    from concourse.bass_utils import run_bass_kernel_spmd

    g = {k: np.asarray(v) for k, v in inputs.items()}
    w_in = g["w_in"]
    part = [w_in[:, :, n * 512:(n + 1) * 512] for n in range(8)]
    w_up = columns(g["w_up"]).reshape(DEPTH, 2, FT, P, UNIT).transpose(0, 2, 1, 3, 4).reshape(DEPTH, 2 * FT, P, UNIT)
    w_out = g["w_out"].reshape(DEPTH, KT, P, UNIT)[:, [4, 5, 6, 7, 0, 1, 2, 3]]
    w_down = g["w_down"].reshape(DEPTH, FT, P, UNIT)
    wts = np.concatenate([columns(part[4]), columns(part[5]), columns(part[3]), two_rows(part[6]),
                          columns(part[0]), columns(part[1]), columns(part[7]), two_rows(part[2]),
                          w_out, w_up, w_down], axis=1).reshape(DEPTH * UNITS, P, UNIT)
    par = np.zeros((DEPTH, P, NR), np.float32)
    par[:, :, R_MIXG:R_MIXG + 8] = g["mix_norm_g"].reshape(DEPTH, KT, P).transpose(0, 2, 1)
    par[:, :, R_FFNG:R_FFNG + 8] = g["ffn_norm_g"].reshape(DEPTH, KT, P).transpose(0, 2, 1)
    for col, name in ((R_QG, "q_norm_g"), (R_KG, "k_norm_g"), (R_LAM, "lam_q1"), (R_LAM + 1, "lam_k1"),
                      (R_LAM + 2, "lam_q2"), (R_LAM + 3, "lam_k2")):
        par[:, :, col] = np.concatenate([g[name], g[name]], axis=1)
    par[:, :, R_DAG] = g["diff_out_g"]
    par[:, :, R_HGG] = g["hg_out_g"]
    conv = np.concatenate([g["conv_w"], g["conv_b"][:, None]], axis=1)
    conv = conv.reshape(DEPTH, 4, 2, FT, P).transpose(0, 4, 3, 2, 1)
    par[:, :, R_CONV:R_CONV + 8 * FT] = conv.reshape(DEPTH, P, 8 * FT)
    lbl = np.ascontiguousarray(g["hg_lb_logits"].reshape(DEPTH, 8, P).transpose(2, 0, 1))
    pos = np.ascontiguousarray(np.broadcast_to(g["positions"].reshape(1, S), (P, S)))
    xT = np.ascontiguousarray(g["x"].reshape(S, KT, P).transpose(2, 1, 0))
    arrays = {"xT": xT, "wts": wts, "cst": constants(), "par": par, "lbl": lbl, "pos": pos}

    nc = bacc.Bacc("TRN2", target_bir_lowering=False, num_devices=1)
    aps = {k: nc.dram_tensor(k, a.shape, mybir.dt.from_np(a.dtype), kind="ExternalInput").ap() for k, a in arrays.items()}
    out = nc.dram_tensor("outT", (P, KT, S), F32, kind="ExternalOutput").ap()
    build(nc, *[aps[k] for k in ("xT", "wts", "cst", "par", "lbl", "pos")], out)
    r = run_bass_kernel_spmd(nc, [arrays], core_ids=[0])
    y = np.asarray(r.results[0]["outT"])
    return np.ascontiguousarray(y.transpose(2, 1, 0)).reshape(1, S, D)
```

```python
from contextlib import ExitStack

import numpy as np
import concourse.bass as bass
from concourse import mybir

F32 = mybir.dt.float32
F32R = mybir.dt.float32r
I32 = mybir.dt.int32
U8 = mybir.dt.uint8
ALU = mybir.AluOpType
ACT = mybir.ActivationFunctionType
AX = mybir.AxisListType

P = 128
D = 1024
S = 512
DEPTH = 2
HEADS = 4
HD = 64
DFF = 2816
EPS = 1e-6
KT = D // P
TT = S // P
FT = DFF // P

UNIT = KT * P
N_IN, N_OUT, N_UP, N_DOWN = 32, 8, 2 * FT, FT
U_OUT = N_IN
U_UP = U_OUT + N_OUT
U_DOWN = U_UP + N_UP
UNITS = U_DOWN + N_DOWN
U_ZF, U_ZB, U_HQ, U_HI, U_DQ, U_DK, U_DV, U_HG = range(0, 32, 4)

LEVELS = 11

ITEMS = 2 * (LEVELS + 1)
STEPS = 16
HEAD_ORDER = [("hg", 0), ("hg", 1), ("da", 0), ("da", 1), ("hg", 2), ("hg", 3), ("da", 2), ("da", 3)]
AHEAD = 8


def schedule():
    order = [("unit", u) for u in range(U_HQ + 2)]
    items = iter(range(ITEMS))
    for u in range(U_HQ + 2, U_HG):
        order.append(("unit", u))
        if u == U_HQ + 2:
            order.append(("prep", 0))
        elif u == U_HQ + 2 + LEVELS + 1:
            order += [("item", next(items)), ("prep", 1)]
        else:
            order.append(("item", next(items)))
    units, posts = iter(range(U_HG, N_IN)), iter(range(8))
    for a in range(STEPS):
        if a in (0, 2, 4, 6):
            order.append(("unit", next(units)))
        post = next(posts) if a > AHEAD else None
        if post is not None:
            order.append(("sum", post))
        order.append(("step", a))
        if a < 7:
            order.append(("item", next(items)))
        if post is not None:
            order.append(("post", post))
    return order + [(kind, p) for p in posts for kind in ("sum", "post")]


ORDER = schedule()

C_IDENT = 0
C_MEAN_D = C_IDENT + P
C_MEAN_H = C_MEAN_D + P
C_ROT = C_MEAN_H + P
C_FREQ = C_ROT + P
C_LAM = C_FREQ + 1
C_OML = C_LAM + DEPTH
C_EPS = C_OML + DEPTH
C_LN8 = C_EPS + 1
NC = C_LN8 + 1

R_MIXG, R_FFNG, R_QG, R_KG, R_DAG, R_HGG = 0, 8, 16, 17, 18, 19
R_LAM = 20
R_CONV = 24
NR = R_CONV + 8 * (FT + 2)


class Chain:

    def __init__(self, eng, sem, base=0):
        self.eng, self.sem, self.base, self.n = eng, sem, base, 0

    def __call__(self, ins):
        ins.then_inc(self.sem, 1)
        self.n += 1
        self.eng.wait_ge(self.sem, self.base + self.n)


def build(nc, xT, wts, cst, msk, par, lbl, pos, outT):
    ctx = ExitStack()
    mix = ExitStack()
    ffn = ExitStack()

    def sb(name, shape, dt=F32, scope=ctx):
        return scope.enter_context(nc.sbuf_tensor(name, shape, dt))

    def sem(name):
        s = ctx.enter_context(nc.semaphore(name))
        layer_sems.append(s)
        return s

    layer_sems = []
    with ctx:
        x = sb("x", [P, KT, S])
        hH = sb("hH", [P, KT, S], F32R)
        hL = sb("hL", [P, KT, S], F32R)
        raw = sb("raw", [P, 2, UNIT])
        wH = sb("wH", [P, 2, UNIT], F32R)
        wL = sb("wL", [P, 2, UNIT], F32R)
        C = sb("C", [P, NC])
        M = sb("M", [P, 7 * P], U8)
        R = sb("R", [P, NR])
        rms = sb("rms", [P, S])
        sq = sb("sq", [P, 2, S])
        rstd = sb("rstd", [P, 2, S])
        tmp = sb("tmp", [P, 2, S])
        rotg = sb("rotg", [P, 2, P])
        lball = sb("lball", [P, DEPTH, 8])
        lb = sb("lb", [P, 8])
        omlb = sb("omlb", [P, 8])
        lamc = sb("lamc", [P, 8])
        dag = sb("dag", [P, 1])
        sm = sb("sm", [P, STEPS, 8])
        cw = sb("cw", [P, 2, 8])
        bank = [ctx.enter_context(nc.psum_tensor(f"bank{i}", [P, S], F32)) for i in range(8)]

        KK = sb("KK", [P, 2, HEADS * S], F32, mix)
        QQ = sb("QQ", [P, 2, HEADS * S], F32, mix)
        T = sb("T", [P, 2, HEADS * S], F32, mix)
        A = sb("A", [P, 2, TT, S], F32, mix)
        HI = sb("HI", [P, TT, S], F32, mix)
        V = sb("V", [P, TT, S], F32, mix)
        QK = sb("QK", [P, 8, S], F32, mix)
        E = sb("E", [P, 2, S], F32, mix)
        wT = sb("wT", [P, 2, TT, P], F32, mix)
        kx = sb("kx", [P, 2, S], F32, mix)
        ev = sb("ev", [P, 2, S], F32, mix)
        W = sb("W", [P, S], F32, mix)
        mix.close()
        gH = sb("gH", [P, FT * S], F32R, ffn)
        gL = sb("gL", [P, FT * S], F32R, ffn)
        uu = sb("uu", [P, 2, 2, S], F32, ffn)
        ua = sb("ua", [P, 2, S], F32, ffn)
        uv = sb("uv", [P, 2, S], F32, ffn)
        gt = sb("gt", [P, 2, S], F32, ffn)
        ffn.close()
        Af = A[:].rearrange("p h s t -> p (h s t)")
        sp = Af[:, 0:2 * S].rearrange("p (b t) -> p b t", b=2)
        sn = Af[:, 2 * S:4 * S].rearrange("p (b t) -> p b t", b=2)
        tt = Af[:, 4 * S:5 * S]
        ang, turns, big, wrap = (V[:, n, :] for n in range(4))
        cosT, sinT = E[:, 0, :], E[:, 1, :]
        posi = QK[:, 7, :].bitcast(I32)

        par_in = sem("par_in")
        pos_in = sem("pos_in")
        raw_in = [sem("raw_in0"), sem("raw_in1")]
        w_high = sem("w_high")
        w_split = sem("w_split")
        w_used = sem("w_used")
        gate_w = sem("gate_w")
        set_up = sem("set_up")
        lam_sum = sem("lam_sum")
        lam_exp = sem("lam_exp")
        x_upd = sem("x_upd")
        sq_ready = sem("sq_ready")
        sq_used = sem("sq_used")
        rms_ln = sem("rms_ln")
        rms_ready = sem("rms_ready")
        hH_ready = sem("hH_ready")
        hL_ready = sem("hL_ready")
        angles = sem("angles")
        tables = sem("tables")
        unit_ev = sem("unit_ev")
        qk_sq = sem("qk_sq")
        qk_aux = sem("qk_aux")
        qk_ln = sem("qk_ln")
        qk_rstd = sem("qk_rstd")
        rope_cr = sem("rope_cr")
        rope_done = sem("rope_done")
        z_sig = sem("z_sig")
        z_done = sem("z_done")
        tok_tr = sem("tok_tr")
        tok_ev = sem("tok_ev")
        gs_done = sem("gs_done")
        hg_q = sem("hg_q")
        hg_k = sem("hg_k")
        kx_ready = sem("kx_ready")
        tot_ready = sem("tot_ready")
        lv_mm = sem("lv_mm")
        a_cp = sem("a_cp")
        a_msk = sem("a_msk")
        av_mm = sem("av_mm")
        oh_ready = sem("oh_ready")
        sc_mm = sem("sc_mm")
        neg_max = sem("neg_max")
        exps = sem("exps")
        w_ready = sem("w_ready")
        tr_mm = sem("tr_mm")
        wT_ready = sem("wT_ready")
        pv_mm = sem("pv_mm")
        od_ready = sem("od_ready")
        o_sq = sem("o_sq")
        o_sum = sem("o_sum")
        o_ln = sem("o_ln")
        o_rstd = sem("o_rstd")
        y_ready = sem("y_ready")
        yH_ready = sem("yH_ready")
        yL_ready = sem("yL_ready")
        wo_done = sem("wo_done")
        up_ev = sem("up_ev")
        conv_init = sem("conv_init")
        conv_done = sem("conv_done")
        silu_done = sem("silu_done")
        g_ready = sem("g_ready")
        gH_ready = sem("gH_ready")
        gL_ready = sem("gL_ready")
        gate_a = sem("gate_a")
        wd_done = sem("wd_done")
        dve_own = sem("dve_own")
        dve_ffn = sem("dve_ffn")
        pre_in = ctx.enter_context(nc.semaphore("pre_in"))
        pre_dve = ctx.enter_context(nc.semaphore("pre_dve"))
        pre_act = ctx.enter_context(nc.semaphore("pre_act"))
        x_in = [ctx.enter_context(nc.semaphore(f"x_in{k}")) for k in range(KT)]
        out_done = ctx.enter_context(nc.semaphore("out_done"))

        def cst_at(c, n=P):
            return C[:, c:c + n]

        def blocks(v, h):
            return v.rearrange("p (n two h) -> p n two h", two=2, h=h)

        def head(t, plane, hd, i=0, n=TT):
            return t[:, plane, hd * S + i * P:hd * S + (i + n) * P]

        def diag(r):
            return bass.AP(tensor=A[:].tensor, offset=r * TT * S, ap=[[2 * TT * S, P], [S + P, TT], [1, P]])

        def gs(hd):
            return T[:, hd // 2, (hd % 2) * 2 * S + S:(hd % 2) * 2 * S + 2 * S]

        def totals(pair, h):
            if h == 1:
                return T[:, :, pair * 2 * S:(pair + 1) * 2 * S]
            if h == 2:
                return wT[:].rearrange("p a k q -> p a (k q)")
            at = pair * 2 * S + S - 4 * S // h
            return T[:, :, at:at + 2 * S // h]

        def token_head(u):
            if U_HI < u <= U_DQ:
                return u - 1 - U_HI
            if U_DV < u <= U_HG:
                return u - 1 - U_DV + 4
            return None

        def score_bank(a, c):
            return bank[(2 if a > AHEAD and a % 2 else 4) + c]

        def scores_after(n):
            return [a for a in ((n + 1,) if n < AHEAD else (n + 1, n + 2) if n == AHEAD else (n + 2,)) if a < STEPS]

        def crossing(t, hd, i, h, left, n=1):
            side = HEADS * S * (1 if left == 0 else -1)
            return bass.AP(tensor=t[:].tensor, offset=left * HEADS * S + hd * S + i * P,
                           ap=[[2 * HEADS * S, P], [2 * h, n * P // (2 * h)], [side + h, 2], [1, h]])

        def out_head(p):
            kind, hd = HEAD_ORDER[p]
            return head(QQ, 0, hd) if kind == "hg" else QK[:, hd, :]

        lraw, le, lp = sm[:, 0:2, :], sm[:, 2:4, :], sm[:, 4:6, :]
        lmax, lsum = sm[:, 6, :], sm[:, 7, :]
        msk32 = KK[:, 0, 0:7 * P].bitcast(I32)
        with nc.Block() as block:
            @block.sync
            def _(sp_):
                for k in range(KT):
                    sp_.dma_start(x[:, k, :], xT[:, k, :]).then_inc(x_in[k], 16)
                sp_.dma_start(msk32, msk).then_inc(pre_in, 16)
                sp_.wait_ge(pre_in, 48)

            @block.vector
            def _(dve):
                ch = Chain(dve, pre_dve)
                dve.wait_ge(pre_in, 48)
                ch(dve.tensor_copy(lmax, lraw[:, 0, :]))
                for l in range(1, DEPTH):
                    ch(dve.tensor_tensor(lmax, lmax, lraw[:, l, :], ALU.max))
                for l in range(DEPTH):
                    ch(dve.tensor_tensor(le[:, l, :], lraw[:, l, :], lmax, ALU.subtract))
                dve.wait_ge(pre_act, 1)
                ch(dve.tensor_copy(lsum, le[:, 0, :]))
                for l in range(1, DEPTH):
                    ch(dve.tensor_tensor(lsum, lsum, le[:, l, :], ALU.add))
                ch(dve.reciprocal(lsum, lsum))
                for l in range(DEPTH):
                    ch(dve.tensor_tensor(lp[:, l, :], le[:, l, :], lsum, ALU.mult))
                ch(dve.tensor_copy(lmax, lp[:, 0, :]))
                for l in range(DEPTH):
                    if l:
                        ch(dve.tensor_tensor(lmax, lmax, lp[:, l, :], ALU.add))
                    ch(dve.tensor_tensor(lball[:, l, :], lmax, lp[:, 0, :], ALU.subtract))
                    ch(dve.tensor_scalar(lball[:, l, :], lball[:, l, :], 0.0, 1.0 - 1e-4, ALU.max, ALU.min))
                ch(dve.tensor_copy(M[:], msk32))

            @block.scalar
            def _(act):
                act.dma_start(lraw, lbl).then_inc(pre_in, 16)
                act.dma_start(C[:], cst).then_inc(pre_in, 16)
                act.wait_ge(pre_dve, 2 * DEPTH)
                act.activation(le, le, ACT.Exp).then_inc(pre_act, 1)

        with nc.Fori(0, DEPTH) as layer:
            with nc.Block() as block:
                @block.sync
                def _(sp_):
                    sp_.dma_start(R[:], par[bass.ds(layer, 1)].rearrange("a p n -> (a p) n")).then_inc(par_in, 16)

                    def load(s, row):
                        sp_.dma_start(raw[:, s, :], wts[bass.ds(row, 1)].rearrange("a p n -> (a p) n"))\
                           .then_inc(raw_in[s], 16)

                    for s in range(2):
                        load(s, layer * UNITS + s)
                    sp_.dma_start(posi, pos).then_inc(pos_in, 16)
                    with sp_.Fori(1, UNITS // 2) as j:
                        for s in range(2):
                            row = layer * UNITS + j * 2 + s
                            sp_.wait_ge(w_split, j * 2 + s - 1)
                            load(s, row)

                @block.gpsimd
                def _(pool):
                    def split(u, s):
                        pool.wait_ge(w_high, u + 1)
                        pool.tensor_tensor(wL[:, s, :], raw[:, s, :], wH[:, s, :].bitcast(F32), ALU.subtract)\
                            .then_inc(w_split, 1)

                    def split_now(u):
                        if u < UNITS:
                            split(u, u % 2)

                    def grow(pair, lv):
                        h = 2 ** (lv - 1)
                        tot = totals(pair, h)
                        pool.wait_ge(lv_mm, 22 * pair + 2 * lv + 2)
                        pool.wait_ge(hg_q, 10 * pair + lv + 1)
                        if pair + lv > 1:
                            pool.wait_ge(hg_k, 8 * pair + lv - 1)
                        if lv == 2:
                            pool.wait_ge(tot_ready, 7 * pair + 1)
                        if 1 < h < 128:
                            for d in range(2):
                                w = tot[:, d, :].rearrange("p (n two) -> p n two", two=2)
                                nxt = pool.tensor_tensor(totals(pair, 2 * h)[:, d, :], w[:, :, 0], w[:, :, 1], ALU.mult)
                            nxt.then_inc(tot_ready, 1)
                        n = S // h
                        for half in range(2):
                            v = blocks(KK[:, half, pair * 2 * S:(pair + 1) * 2 * S], h)[:, :, half, :]
                            w = tot[:, half, :].rearrange("p (n two o) -> p n two o", two=2, o=1)[:, :, 1 - half, :]
                            last = pool.tensor_tensor(v, v, w.to_broadcast([P, n, h]), ALU.mult)
                        last.then_inc(hg_k, 1)

                    def square(p):
                        kind, hd = HEAD_ORDER[p]
                        pool.wait_ge(*((oh_ready, hd + 1) if kind == "hg" else (od_ready, hd + 1)))
                        if p >= 2:
                            pool.wait_ge(o_sum, p - 1)
                        pool.tensor_tensor(sq[:, p % 2, :], out_head(p), out_head(p), ALU.mult).then_inc(o_sq, 1)

                    def post(p):
                        t = tmp[:, p % 2, :]
                        pool.wait_ge(y_ready, p + 1)
                        pool.tensor_scalar(hH[:, p, :], t, 1.0, 1.0, ALU.mult, ALU.mult).then_inc(yH_ready, 1)
                        pool.wait_ge(yH_ready, p + 1)
                        pool.tensor_tensor(hL[:, p, :], t, hH[:, p, :].bitcast(F32), ALU.subtract).then_inc(yL_ready, 1)

                    for kind, n in ORDER:
                        if kind == "unit":
                            if n == 0:
                                split_now(0)
                                split_now(1)
                            split_now(n + 2)
                        elif kind == "item":
                            pair, lv = divmod(n, LEVELS + 1)
                            if 1 <= lv <= 8:
                                grow(pair, lv)
                            if n == ITEMS - 1:
                                square(0)
                                square(1)
                        elif kind == "post":
                            post(n)
                            if n + 2 < 8:
                                square(n + 2)
                    with pool.Fori(N_IN // 2 + 1, UNITS // 2) as j:
                        for s in range(2):
                            split(j * 2 + s, s)

                @block.tensor
                def _(pe):
                    def triple(out, s, a, rhs_h, rhs_l, first, last):
                        pe.matmul(out, wH[:, s, a:a + P], rhs_h, start=first, stop=False)
                        pe.matmul(out, wL[:, s, a:a + P], rhs_h, start=False, stop=False)
                        return pe.matmul(out, wH[:, s, a:a + P], rhs_l, start=False, stop=last)

                    def column(u, out, norm=None):
                        pe.wait_ge(w_split, u + 1)
                        for k in range(KT):
                            if norm is not None:
                                if norm and k == 0:
                                    pe.wait_ge(x_upd, 3)
                                pe.wait_ge(sq_ready, 8 * norm + k + 1)
                                pe.matmul(bank[2][:], cst_at(C_MEAN_D), sq[:, k % 2, :], start=k == 0,
                                          stop=k == KT - 1).then_inc(sq_used, 1)
                                pe.wait_ge(hL_ready, 8 * norm + k + 1)
                            m = triple(out, u % 2, k * P, hH[:, k, :], hL[:, k, :], k == 0, k == KT - 1)
                        m.then_inc(w_used, 1)

                    def unit(u):
                        if u >= 2:
                            pe.wait_ge(unit_ev, u - 1)
                        column(u, bank[u % 2][:], 0 if u == 0 else None)
                        if U_DQ < u <= U_DV:
                            aux(u - 1 - U_DQ)
                        if token_head(u) is not None:
                            to_tokens(token_head(u))

                    def aux(n):
                        pe.wait_ge(qk_sq, n + 1)
                        if n:
                            pe.wait_ge(qk_ln, n)
                            pe.wait_ge(rope_cr, n)
                        else:
                            pe.wait_ge(set_up, 2)
                            pe.wait_ge(tok_ev, 4)
                        pe.matmul(bank[6][:], cst_at(C_MEAN_H), sq[:, n % 2, :], start=True, stop=True)
                        pe.matmul(bank[7][:], rotg[:, n // 4, :], QK[:, n, :], start=True, stop=True).then_inc(qk_aux, 1)

                    def to_tokens(n):
                        pe.wait_ge(unit_ev, (U_HI if n < 4 else U_DV - 4) + n + 1)
                        if n == 4:
                            pe.wait_ge(qk_ln, 8)
                            pe.wait_ge(rope_cr, 8)
                        if n >= 2:
                            pe.wait_ge(tok_ev, n - 1)
                        for i in range(TT):
                            m = pe.transpose(bank[6 + n % 2][:, i * P:i * P + P], ev[:, n % 2, i * P:i * P + P],
                                             cst_at(C_IDENT))
                        m.then_inc(tok_tr, 1)

                    def item(n):
                        pair, lv = divmod(n, LEVELS + 1)
                        if lv == LEVELS:
                            pe.wait_ge(tok_ev, 4)
                            for r in range(2):
                                hd = 2 * pair + r
                                pe.wait_ge(a_cp, 8 * pair + 6 + r + 1)
                                for i in range(TT):
                                    m = pe.matmul(bank[2 + r][:], HI[:, i, hd * P:hd * P + P], A[:, r, i, :],
                                                  start=i == 0, stop=i == TT - 1)
                                m.then_inc(av_mm, 1)
                            return
                        pe.wait_ge(hg_q, 10 * pair + min(lv, 9) + 1)
                        if 1 <= lv <= 7:
                            pe.wait_ge(kx_ready, 7 * pair + lv)
                        elif lv:
                            pe.wait_ge(hg_k, 8 * pair + min(lv, 9) - 1)
                        for r in range(2):
                            hd, b = 2 * pair + r, bank[2 + r]
                            if lv == 0:
                                if pair:
                                    pe.wait_ge(oh_ready, r + 1)
                                else:
                                    pe.wait_ge(rms_ln, 1)
                            elif lv == 1 or lv > 8:
                                pe.wait_ge(a_cp, 8 * pair + (0 if lv == 1 else 2 * (lv - 8)) + r + 1)
                            else:
                                pe.wait_ge(a_msk, 14 * pair + 2 * (lv - 2) + r + 1)
                            if lv <= 8:
                                for i in range(TT):
                                    o = b[:, i * P:i * P + P]
                                    if lv == 0:
                                        m = pe.matmul(o, kx[:, r, i * P:i * P + P], head(QQ, 1, hd, i, 1),
                                                      start=True, stop=True)
                                    elif lv < 8:
                                        h = 2 ** (lv - 1)
                                        m = pe.matmul(o.rearrange("p (n two h) -> p n two h", two=2, h=h),
                                                      kx[:, r, i * P:i * P + P], crossing(QQ, hd, i, h, 0),
                                                      start=True, stop=True)
                                    else:
                                        m = pe.matmul(o, head(KK, i % 2, hd, i, 1), head(QQ, 1 - i % 2, hd, i ^ 1, 1),
                                                      start=True, stop=True)
                            else:
                                half = lv - 9
                                for i in range(2):
                                    m = pe.matmul(b[:, i * 2 * P:(i + 1) * 2 * P], head(KK, half, hd, 2 * half + i, 1),
                                                  head(QQ, 1 - half, hd, 2 - 2 * half, 2), start=True, stop=True)
                            m.then_inc(lv_mm, 1)

                    def scores(a):
                        hd, qt = divmod(a, 4)
                        if a == 0:
                            pe.wait_ge(rope_done, 8)
                        elif a <= AHEAD:
                            pe.wait_ge(exps, a)
                        elif a == AHEAD + 1:
                            pe.wait_ge(oh_ready, 4)
                        else:
                            pe.wait_ge(exps, a - 1)
                        for c in range(2):
                            r = slice(HD * c, HD * c + HD)
                            m = pe.matmul(score_bank(a, c)[:], QK[r, hd, qt * P:qt * P + P], QK[r, 4 + hd, :],
                                          start=True, stop=True)
                        m.then_inc(sc_mm, 1)

                    def turn(a):
                        if a == 0:
                            pe.wait_ge(tok_ev, 7)
                        else:
                            pe.wait_ge(wT_ready, a)
                        pe.wait_ge(w_ready, a + 1)
                        for k in range(TT):
                            m = pe.transpose(bank[6][:, k * P:k * P + P], W[:, k * P:k * P + P], cst_at(C_IDENT))
                        m.then_inc(tr_mm, 1)

                    def values(a):
                        hd, qt = divmod(a, 4)
                        pe.wait_ge(wT_ready, a + 1)
                        if a == 0:
                            pe.wait_ge(tok_ev, 8)
                        elif qt == 0:
                            pe.wait_ge(od_ready, hd)
                        for k in range(TT):
                            m = pe.matmul(bank[7][:, qt * P:qt * P + P], V[:, k, hd * P:hd * P + P], wT[:, a % 2, k, :],
                                          start=k == 0, stop=k == TT - 1)
                        m.then_inc(pv_mm, 1)

                    def post(p):
                        pe.wait_ge(o_sq, p + 1)
                        if p:
                            pe.wait_ge(o_ln, p)
                        else:
                            pe.wait_ge(unit_ev, N_IN)
                        pe.matmul(bank[1][:], cst_at(C_MEAN_D), sq[:, p % 2, :], start=True, stop=True).then_inc(o_sum, 1)

                    pe.wait_ge(set_up, 1)
                    pe.matmul(bank[3][:, 0:2], cst_at(C_MEAN_D), lamc[:, 0:2], start=True, stop=True).then_inc(lam_sum, 1)
                    prev = None
                    for kind, n in ORDER:
                        if kind == "unit":
                            unit(n)
                            if n == U_HG - 1:
                                scores(0)
                        elif kind == "item":
                            if n == 0:
                                pe.wait_ge(lam_exp, 1)
                            item(n)
                        elif kind == "step":
                            for a in scores_after(n):
                                scores(a)
                            if n:
                                values(n - 1)
                            turn(n)
                        elif kind == "sum":
                            if n < KT - 1:
                                post(n)
                            else:
                                values(STEPS - 1)

                    for p in range(KT):
                        u = U_OUT + p
                        pe.wait_ge(w_split, u + 1)
                        pe.wait_ge(yL_ready, p + 1)
                        for n, m_ in enumerate((0, 2, 3, 4, 5, 6, 7, 1)):
                            if p == 0 and m_ == 7:
                                pe.wait_ge(od_ready, 4)
                            if p == 0 and m_ == 1:
                                post(KT - 1)
                                pe.wait_ge(o_ln, 8)
                            if p == KT - 1:
                                m_ = n
                            m = triple(bank[m_][:], u % 2, m_ * P, hH[:, p, :], hL[:, p, :], p == 0, p == KT - 1)
                            if p == KT - 1 and m_ < KT - 1:
                                m.then_inc(wo_done, 1)
                        m.then_inc(w_used, 1)

                    pe.wait_ge(x_upd, 1)

                    def pair(i, q, first):
                        for c in range(2):
                            b = bank[2 * q + c]
                            if first:
                                if q == 0 and c == 1:
                                    pe.wait_ge(x_upd, 2)
                                if q == 1:
                                    pe.wait_ge(x_upd, 8)
                                    pe.wait_ge(rms_ln, 2)
                                column(U_UP + 2 * q + c, b[:], 1 if q == 0 and c == 0 else None)
                                continue
                            pe.wait_ge(w_split, i * 4 + (U_UP + 2 * q + c + 1))
                            pe.wait_ge(up_ev, i * 4 + (2 * (q - 2) + c + 1))
                            for k in range(KT):
                                m = triple(b[:], c, k * P, hH[:, k, :], hL[:, k, :], k == 0, k == KT - 1)
                            m.then_inc(w_used, 1)

                    for q in range(2):
                        pair(0, q, True)
                    with pe.Fori(1, FT // 2) as i:
                        for q in range(2):
                            pair(i, q, False)

                    def down(k, s, gh, gl, first, last):
                        pe.wait_ge(w_split, k + (U_DOWN + 1))
                        pe.wait_ge(gL_ready, k + 1)
                        for n in range(KT):
                            m_ = n if last else (n + 4) % KT
                            if first and m_ == 0:
                                pe.wait_ge(up_ev, 2 * FT)
                            m = triple(bank[m_][:], s, m_ * P, gh, gl, first, last)
                            if last and m_ < KT - 1:
                                m.then_inc(wd_done, 1)
                        m.then_inc(w_used, 1)

                    for k in range(2):
                        down(k, k, gH[:, k * S:(k + 1) * S], gL[:, k * S:(k + 1) * S], k == 0, False)
                    with pe.Fori(1, FT // 2 - 1) as i:
                        for s in range(2):
                            down(i * 2 + s, s, gH[:, bass.ds(i * (2 * S) + s * S, S)],
                                 gL[:, bass.ds(i * (2 * S) + s * S, S)], False, False)
                    for k in range(FT - 2, FT):
                        down(k, k % 2, gH[:, k * S:(k + 1) * S], gL[:, k * S:(k + 1) * S], False, k == FT - 1)

                @block.scalar
                def _(act):
                    eps = cst_at(C_EPS, 1)

                    def high(u, s, turn, first=False, looped=False):
                        act.wait_ge(raw_in[s], turn)
                        if not first:
                            act.wait_ge(w_used, u - 1)
                        if looped:
                            act.sem_inc(gate_w, 1)
                        act.activation(wH[:, s, :], raw[:, s, :], ACT.Copy).then_inc(w_high, 1)

                    def high_now(u):
                        high(u, u % 2, 16 * (u // 2 + 1), u < 2)

                    def prepare(n, col):
                        for k in range(KT):
                            if n:
                                act.wait_ge(x_upd, k + 1)
                                if k == KT - 1:
                                    act.wait_ge(w_used, U_UP)
                            else:
                                act.wait_ge(x_in[k], 16)
                                if k == 0:
                                    act.wait_ge(par_in, 16)
                            act.activation(hH[:, k, :], x[:, k, :], ACT.Identity,
                                           scale=R[:, col + k:col + k + 1]).then_inc(hH_ready, 1)
                            if k >= 2:
                                act.wait_ge(sq_used, 8 * n + k - 1)
                            act.activation(sq[:, k % 2, :], x[:, k, :], ACT.Square).then_inc(sq_ready, 1)
                            if n == 0 and k in (0, 4):
                                high_now(k // 4)
                            if n == 1 and k == 4:
                                high_now(U_UP + 1)
                        act.wait_ge(sq_used, 8 * n + 8)
                        act.activation(rms[:], bank[2][:], ACT.Ln, bias=eps).then_inc(rms_ln, 1)
                        act.wait_ge(rms_ln, n + 1)
                        act.activation(rms[:], rms[:], ACT.Exp, scale=-0.5).then_inc(rms_ready, 1)

                    def logs():
                        nc.scalar.preload_act_table_set("natural_log_exp_and_others")

                    logs()
                    prepare(0, R_MIXG)
                    act.wait_ge(lam_sum, 1)
                    act.activation(lamc[:, 2:4], bank[3][:, 0:2], ACT.Exp, scale=0.5 * D).then_inc(lam_exp, 1)

                    def rope_stats(n):
                        act.wait_ge(qk_aux, n + 1)
                        if n >= 2:
                            act.wait_ge(rope_done, n - 1)
                        r = rstd[:, n % 2, :]
                        act.activation(r, bank[6][:], ACT.Ln, bias=eps).then_inc(qk_ln, 1)
                        act.wait_ge(qk_ln, n + 1)
                        act.activation(r, r, ACT.Exp, scale=-0.5,
                                       bias=cst_at(C_LN8, 1) if n < 4 else 0.0).then_inc(qk_rstd, 1)

                    def tokens(n):
                        act.wait_ge(tok_tr, n + 1)
                        dst = HI if n < 4 else V
                        act.activation(dst[:, :, (n % 4) * P:(n % 4 + 1) * P],
                                       bank[6 + n % 2][:].rearrange("p (i c) -> p i c", i=TT), ACT.Copy)\
                            .then_inc(tok_ev, 1)

                    def unit(u):
                        high_now(u + 2)
                        if U_DQ < u <= U_DV:
                            rope_stats(u - 1 - U_DQ)
                        if token_head(u) is not None:
                            tokens(token_head(u))
                        if u < U_HQ:
                            act.wait_ge(unit_ev, u + 1)
                            if u >= U_ZF + 2:
                                act.wait_ge(z_done, u - U_ZF - 1)
                            act.activation(sp[:, u % 2, :], ev[:, u % 2, :], ACT.Sigmoid)
                            act.activation(sn[:, u % 2, :], ev[:, u % 2, :], ACT.Sigmoid, scale=-1.0).then_inc(z_sig, 1)
                        elif u == U_HI + 1:
                            act.wait_ge(angles, 1)
                            act.activation(cosT, turns, ACT.Sin)
                            act.activation(sinT, ang, ACT.Sin).then_inc(tables, 1)
                            logs()
                        elif U_DQ <= u < U_DV:
                            n = u - U_DQ
                            act.wait_ge(unit_ev, u + 1)
                            if n >= 2:
                                act.wait_ge(qk_aux, n - 1)
                            act.activation(sq[:, n % 2, :], QK[:, n, :], ACT.Square).then_inc(qk_sq, 1)
                        elif u == N_IN - 1:
                            for hd in range(HEADS):
                                act.wait_ge(unit_ev, U_HG + hd + 1)
                                act.activation(gs(hd), gs(hd), ACT.Silu).then_inc(gs_done, 1)
                            logs()

                    def item(n):
                        pair, lv = divmod(n, LEVELS + 1)
                        for r in range(2):
                            if lv == LEVELS:
                                act.wait_ge(av_mm, 2 * pair + r + 1)
                                act.activation(head(QQ, 0, 2 * pair + r), bank[2 + r][:], ACT.Copy).then_inc(oh_ready, 1)
                                continue
                            if 1 <= lv <= 7:
                                continue
                            act.wait_ge(lv_mm, 22 * pair + 2 * lv + r + 1)
                            b = bank[2 + r][:].rearrange("p (i t) -> p i t", i=TT)
                            if lv == 0:
                                if pair:
                                    act.wait_ge(av_mm, r + 1)
                                act.activation(diag(r), b, ACT.Copy).then_inc(a_cp, 1)
                            elif lv == 8:
                                base, row = r * TT * S, 2 * TT * S
                                for o in range(2):
                                    dst = bass.AP(tensor=A[:].tensor, offset=base + (P if o == 0 else S),
                                                  ap=[[row, P], [2 * S + 2 * P, 2], [1, P]])
                                    cp = act.activation(dst, b[:, o::2, :], ACT.Copy)
                                cp.then_inc(a_cp, 1)
                            else:
                                half = lv - 9
                                act.activation(A[:, r, 2 * half:2 * half + 2, (2 - 2 * half) * P:(4 - 2 * half) * P],
                                               bank[2 + r][:].rearrange("p (i t) -> p i t", i=2), ACT.Copy)\
                                    .then_inc(a_cp, 1)

                        if lv <= 6:
                            act.wait_ge(lv_mm, 22 * pair + 2 * lv + 2)
                            if lv:
                                act.wait_ge(hg_k, 8 * pair + lv)
                            h = 2 ** lv
                            act.activation(kx[:].rearrange("p r t -> p (r t)").rearrange("p (n two h) -> p n two h", two=2, h=h),
                                           crossing(KK, 2 * pair, 0, h, 0, 2 * TT), ACT.Copy).then_inc(kx_ready, 1)

                    def back(a):
                        act.wait_ge(tr_mm, a + 1)
                        if a == 0:
                            act.wait_ge(hg_q, 10 + 4)
                            act.wait_ge(hg_k, 8 + 2)
                            act.wait_ge(tot_ready, 7 + 2)
                        if a >= 2:
                            act.wait_ge(pv_mm, a - 1)
                        act.activation(wT[:, a % 2, :, :], bank[6][:].rearrange("p (k q) -> p k q", k=TT), ACT.Copy)\
                            .then_inc(wT_ready, 1)

                    def exponentials(a):
                        act.wait_ge(neg_max, a + 1)
                        if a == 0:
                            act.wait_ge(rope_cr, 8)
                        else:
                            act.wait_ge(w_ready, a)
                        for c in range(2):
                            e = act.activation(E[:, c, :], score_bank(a, c)[:], ACT.Exp,
                                               bias=sm[:, a, c:c + 1], accum_out=sm[:, a, 2 + c:3 + c])
                        e.then_inc(exps, 1)

                    def head_out(hd):
                        act.wait_ge(pv_mm, 4 * hd + 4)
                        act.activation(QK[:, hd, :], bank[7][:], ACT.Copy).then_inc(od_ready, 1)

                    def post(p):
                        act.wait_ge(o_sum, p + 1)
                        if p >= 2:
                            act.wait_ge(y_ready, p - 1)
                        r = rstd[:, p % 2, :]
                        act.activation(r, bank[1][:], ACT.Ln, bias=eps, scale=float(D // P)).then_inc(o_ln, 1)
                        act.wait_ge(o_ln, p + 1)
                        act.activation(r, r, ACT.Exp, scale=-0.5).then_inc(o_rstd, 1)

                    for kind, n in ORDER:
                        if kind == "unit":
                            unit(n)
                            if n == U_HG - 1:
                                exponentials(0)
                        elif kind == "item":
                            item(n)
                        elif kind == "step":
                            if n and n % 4 == 0:
                                head_out(n // 4 - 1)
                            if n < AHEAD:
                                back(n)
                            if n + 1 < STEPS:
                                exponentials(n + 1)
                            if n >= AHEAD:
                                back(n)
                        elif kind == "sum":
                            if HEAD_ORDER[n] == ("da", 3):
                                head_out(3)
                            post(n)

                    for u in range(U_OUT, U_UP - 1):
                        high_now(u + 2)
                    prepare(1, R_FFNG)

                    def pair(i, q, first):
                        for c, dst in enumerate((ua, uv)):
                            u = U_UP + 2 * q + c + 2
                            if first:
                                high_now(u)
                            else:
                                high(i * 4 + u, c, i * 32 + 16 * (u // 2 + 1), looped=True)
                            if not first:
                                act.wait_ge(g_ready, i * 2 + (q - 1))
                            act.wait_ge(up_ev, i * 4 + (2 * q + c + 1))
                            act.activation(dst[:, q, :], uu[:, q, c, :], ACT.Identity, bias=cw[:, q, 4 * c + 3:4 * c + 4],
                                           scale=cw[:, q, 4 * c + 1:4 * c + 2]).then_inc(conv_init, 1)
                        act.wait_ge(conv_done, i * 4 + (2 * q + 1))
                        act.activation(ua[:, q, :], ua[:, q, :], ACT.Silu).then_inc(silu_done, 1)
                        act.wait_ge(g_ready, i * 2 + (q + 1))
                        act.sem_inc(gate_a, 1)
                        cols = gH[:, q * S:q * S + S] if first else gH[:, bass.ds(i * (2 * S) + q * S, S)]
                        act.activation(cols, gt[:, q, :], ACT.Copy).then_inc(gH_ready, 1)

                    for q in range(2):
                        pair(0, q, True)
                    with act.Fori(1, FT // 2) as i:
                        for q in range(2):
                            pair(i, q, False)
                    with act.Fori(U_DOWN // 2 + 1, UNITS // 2) as j:
                        for s in range(2):
                            high(j * 2 + s, s, j * 16 + 16, looped=True)

                @block.vector
                def _(dve):
                    ch = Chain(dve, dve_own)

                    def low(n, k, col):
                        dve.wait_ge(hH_ready, 8 * n + k + 1)
                        dve.scalar_tensor_tensor(hL[:, k, :], x[:, k, :], R[:, col + k:col + k + 1],
                                                 hH[:, k, :].bitcast(F32), ALU.mult, ALU.subtract).then_inc(hL_ready, 1)

                    dve.wait_ge(par_in, 16)
                    lv4 = R[:, R_LAM:R_LAM + 4].rearrange("p (a b) -> p a b", b=2)
                    dve.tensor_tensor(lamc[:, 0:2], lv4[:, :, 0], lv4[:, :, 1], ALU.mult).then_inc(set_up, 1)
                    for k in range(KT):
                        low(0, k, R_MIXG)
                    ch(dve.tensor_copy(lb[:], lball[:].rearrange("p l c -> p (l c)")[:, bass.ds(layer * 8, 8)]))
                    ch(dve.tensor_scalar(omlb[:], lb[:], -1.0, 1.0, ALU.mult, ALU.add))
                    ch(dve.tensor_copy(lamc[:, 4:5], C[:, bass.ds(layer + C_LAM, 1)]))
                    ch(dve.tensor_copy(lamc[:, 5:6], C[:, bass.ds(layer + C_OML, 1)]))
                    ch(dve.tensor_tensor(dag[:], R[:, R_DAG:R_DAG + 1], lamc[:, 5:6], ALU.mult))
                    for c in range(2):
                        m = dve.tensor_scalar(rotg[:, c, :], cst_at(C_ROT), R[:, R_QG + c:R_QG + c + 1], None, ALU.mult)
                    m.then_inc(set_up, 1)

                    def rotary(part):
                        TWO_PI = 2 * np.pi
                        c1 = float(np.floor(TWO_PI * 2 ** 9) / 2 ** 9)
                        c2 = float(np.floor((TWO_PI - c1) * 2 ** 21) / 2 ** 21)
                        c3 = float(np.float32(TWO_PI - c1 - c2))
                        BIG = float(1.5 * 2 ** 23)
                        PI = float(np.nextafter(np.float32(np.pi), np.float32(0)))
                        if part == 0:
                            dve.wait_ge(pos_in, 16)
                            ch(dve.tensor_copy(turns, posi))
                            ch(dve.tensor_scalar(ang, turns, C[:, C_FREQ:C_FREQ + 1], None, ALU.mult))
                            ch(dve.tensor_scalar(turns, ang, float(1 / TWO_PI), BIG, ALU.mult, ALU.add))
                            ch(dve.tensor_scalar(turns, turns, -BIG, None, ALU.add))
                            ch(dve.tensor_scalar(big, turns, 1 / 2048, BIG, ALU.mult, ALU.add))
                            ch(dve.tensor_scalar(big, big, -BIG, 2048.0, ALU.add, ALU.mult))
                            ch(dve.tensor_tensor(turns, turns, big, ALU.subtract))
                        elif part == 1:
                            for c in (c1, c2, c3):
                                ch(dve.scalar_tensor_tensor(ang, big, -c, ang, ALU.mult, ALU.add))
                                ch(dve.scalar_tensor_tensor(ang, turns, -c, ang, ALU.mult, ALU.add))
                        else:
                            ch(dve.tensor_scalar(turns, ang, float(np.pi / 2), None, ALU.add))
                            ch(dve.tensor_scalar(wrap, turns, float(np.pi), -TWO_PI, ALU.is_gt, ALU.mult))
                            ch(dve.tensor_tensor(turns, turns, wrap, ALU.add))
                            ch(dve.tensor_scalar(turns, turns, PI, -PI, ALU.min, ALU.max))
                            dve.tensor_scalar(ang, ang, PI, -PI, ALU.min, ALU.max).then_inc(angles, 1)

                    dve.wait_ge(lam_exp, 1)
                    ch(dve.tensor_tensor(lamc[:, 6:7], lamc[:, 3:4], lamc[:, 2:3], ALU.subtract))
                    ch(dve.tensor_tensor(lamc[:, 7:8], lamc[:, 6:7], lamc[:, 4:5], ALU.subtract))
                    e30 = float(np.exp(30.0))

                    def evict(u):
                        dve.wait_ge(w_used, u + 1)
                        if U_DQ <= u < U_DV:
                            dst = QK[:, u - U_DQ, :]
                        elif U_HQ <= u < U_HI:
                            dst = head(QQ, 1, u - U_HQ)
                        elif u >= U_HG:
                            dst = gs(u - U_HG)
                            dve.wait_ge(hg_q, 10 + 3)
                            dve.wait_ge(hg_k, 8 + 1)
                        else:
                            dst = ev[:, u % 2, :]
                            if U_ZF + 2 <= u < U_HQ:
                                dve.wait_ge(z_sig, u - U_ZF - 1)
                            if U_HI + 2 <= u < U_DQ:
                                dve.wait_ge(tok_tr, u - U_HI - 1)
                            if U_DV <= u < U_HG:
                                dve.wait_ge(tok_tr, u - U_DV + 3)
                        if u == 0:
                            dve.wait_ge(rms_ready, 1)
                        dve.tensor_tensor(dst, bank[u % 2][:], rms[:], ALU.mult).then_inc(unit_ev, 1)

                    def rope(n):
                        dve.wait_ge(unit_ev, U_DQ + n + 1)
                        dve.wait_ge(tables, 1)
                        t, q = tmp[:, n % 2, :], QK[:, n, :]
                        ch(dve.scalar_tensor_tensor(t, q, R[:, R_QG + n // 4:R_QG + n // 4 + 1], cosT, ALU.mult, ALU.mult))
                        dve.wait_ge(qk_aux, n + 1)
                        dve.tensor_tensor(q, bank[7][:], sinT, ALU.mult).then_inc(rope_cr, 1)
                        dve.wait_ge(rope_cr, n + 1)
                        ch(dve.tensor_tensor(q, q, t, ALU.add))
                        dve.wait_ge(qk_rstd, n + 1)
                        dve.tensor_tensor(q, q, rstd[:, n % 2, :], ALU.mult).then_inc(rope_done, 1)

                    def forget(n):
                        d, hd = divmod(n, 4)
                        dve.wait_ge(z_sig, n + 1)
                        if n:
                            dve.wait_ge(z_done, n)
                        s_p, s_n, f = sp[:, n % 2, :], sn[:, n % 2, :], head(T, d, hd)
                        ch(dve.tensor_scalar(tt, s_p, e30, 1.0, ALU.mult, ALU.min))
                        ch(dve.tensor_tensor(tt, tt, s_n, ALU.mult))
                        ch(dve.scalar_tensor_tensor(f, tt, lb[:, n:n + 1], s_p, ALU.mult, ALU.add))
                        ch(dve.tensor_scalar(f, f, 1.0, None, ALU.min))
                        dve.tensor_scalar(head(KK, d, hd), s_n, omlb[:, n:n + 1], None, ALU.mult).then_inc(z_done, 1)

                    def prep(pair):
                        cols = slice(pair * 2 * S, (pair + 1) * 2 * S)
                        if pair:
                            dve.wait_ge(lv_mm, 2 * 7 + 2)
                        dve.wait_ge(z_done, 8)
                        ch(dve.tensor_tensor(kx[:].rearrange("p a t -> p (a t)"), KK[:, 0, cols], KK[:, 1, cols], ALU.add))
                        dve.wait_ge(unit_ev, U_HQ + 2 * pair + 2)
                        dve.tensor_tensor(QQ[:, 0, cols], QQ[:, 1, cols], T[:, 1, cols], ALU.mult).then_inc(hg_q, 1)

                    def item(n):
                        pair, lv = divmod(n, LEVELS + 1)
                        cols = slice(pair * 2 * S, (pair + 1) * 2 * S)
                        if lv == 0:
                            dve.wait_ge(hg_q, 10 * pair + 1)
                            dve.wait_ge(lv_mm, 22 * pair + 2)
                            dve.tensor_tensor(QQ[:, 1, cols], QQ[:, 1, cols], T[:, 0, cols], ALU.mult).then_inc(hg_q, 1)
                        if 1 <= lv <= 7:
                            m = M[:, (lv - 1) * P:lv * P].rearrange("p (o t) -> p o t", o=1).to_broadcast([P, TT, P])
                            for r in range(2):
                                dve.wait_ge(lv_mm, 22 * pair + 2 * lv + r + 1)
                                if lv == 1:
                                    dve.wait_ge(a_cp, 8 * pair + r + 1)
                                else:
                                    dve.wait_ge(a_msk, 14 * pair + 2 * (lv - 2) + r + 1)
                                dve.copy_predicated(diag(r), m, bank[2 + r][:].rearrange("p (i t) -> p i t", i=TT))\
                                   .then_inc(a_msk, 1)
                        if 1 <= lv <= 8:
                            h = 2 ** (lv - 1)
                            dve.wait_ge(lv_mm, 22 * pair + 2 * lv + 2)
                            dve.wait_ge(hg_q, 10 * pair + lv + 1)
                            if lv > 1:
                                dve.wait_ge(tot_ready, 7 * pair + lv - 1)
                            for half in range(2):
                                v = blocks(QQ[:, half, cols], h)[:, :, half, :]
                                w = totals(pair, h)[:, 1 - half, :].rearrange("p (n two o) -> p n two o", two=2, o=1)
                                last = dve.tensor_tensor(v, v, w[:, :, 1 - half, :].to_broadcast([P, S // h, h]), ALU.mult)
                            last.then_inc(hg_q, 1)
                        if lv == 1:
                            if pair:
                                dve.wait_ge(hg_k, 8)
                            for d in range(2):
                                w = totals(pair, 1)[:, d, :].rearrange("p (n two) -> p n two", two=2)
                                nxt = dve.tensor_tensor(totals(pair, 2)[:, d, :], w[:, :, 0], w[:, :, 1], ALU.mult)
                            nxt.then_inc(tot_ready, 1)

                    def row_max(a):
                        dve.wait_ge(sc_mm, a + 1)
                        for c in range(2):
                            m = dve.tensor_reduce(sm[:, a, c:c + 1], score_bank(a, c)[:], axis=AX.X, op=ALU.max, negate=True)
                        m.then_inc(neg_max, 1)

                    def combine(a):
                        dve.wait_ge(exps, a + 1)
                        ch(dve.reciprocal(sm[:, a, 4:6], sm[:, a, 2:4]))
                        ch(dve.tensor_tensor(sm[:, a, 6:7], sm[:, a, 5:6], lamc[:, 7:8], ALU.mult))
                        ch(dve.tensor_scalar(E[:, 0, :], E[:, 0, :], sm[:, a, 4:5], None, ALU.mult))
                        if a:
                            dve.wait_ge(tr_mm, a)
                        dve.scalar_tensor_tensor(W[:], E[:, 1, :], sm[:, a, 6:7], E[:, 0, :], ALU.mult, ALU.add)\
                           .then_inc(w_ready, 1)

                    def post(p):
                        kind, hd = HEAD_ORDER[p]
                        dve.wait_ge(o_rstd, p + 1)
                        if p >= 2:
                            dve.wait_ge(yL_ready, p - 1)
                        t = tmp[:, p % 2, :]
                        if kind == "hg":
                            ch(dve.scalar_tensor_tensor(t, out_head(p), R[:, R_HGG:R_HGG + 1], rstd[:, p % 2, :],
                                                        ALU.mult, ALU.mult))
                            dve.wait_ge(gs_done, hd + 1)
                            dve.tensor_tensor(t, t, gs(hd), ALU.mult).then_inc(y_ready, 1)
                        else:
                            dve.scalar_tensor_tensor(t, out_head(p), dag[:, 0:1], rstd[:, p % 2, :],
                                                     ALU.mult, ALU.mult).then_inc(y_ready, 1)

                    for kind, n in ORDER:
                        if kind == "unit":
                            evict(n)
                            if U_ZF < n <= U_HQ:
                                forget(n - U_ZF - 1)
                            if n == U_HQ + 1:
                                rotary(0)
                            if n == U_HI:
                                rotary(2)
                            if U_DQ < n <= U_DV:
                                rope(n - 1 - U_DQ)
                            if n == U_HG - 1:
                                row_max(0)
                        elif kind == "prep":
                            prep(n)
                            if n == 0:
                                rotary(1)
                        elif kind == "item":
                            item(n)
                        elif kind == "step":
                            combine(n)
                            for a in scores_after(n):
                                row_max(a)
                        elif kind == "post":
                            post(n)

                    for m_ in range(KT):
                        if m_ < KT - 1:
                            dve.wait_ge(wo_done, m_ + 1)
                        else:
                            dve.wait_ge(w_used, U_UP)
                        dve.tensor_tensor(x[:, m_, :], x[:, m_, :], bank[m_][:], ALU.add).then_inc(x_upd, 1)
                        if m_ >= 1:
                            low(1, m_ - 1, R_FFNG)
                    low(1, KT - 1, R_FFNG)
                    for q in range(2):
                        ch(dve.tensor_copy(cw[:, q, :], R[:, R_CONV + 8 * q:R_CONV + 8 * q + 8]))
                    dve.wait_ge(rms_ready, 2)

                    def pair(i, q, first, own):
                        for c in range(2):
                            dve.wait_ge(w_used, i * 4 + (U_UP + 2 * q + c + 1))
                            dve.tensor_tensor(uu[:, q, c, :], bank[2 * q + c][:], rms[:], ALU.mult).then_inc(up_ev, 1)
                        for c, dst in enumerate((ua, uv)):
                            w = lambda n: cw[:, q, 4 * c + n:4 * c + n + 1]
                            dve.wait_ge(conv_init, i * 4 + (2 * q + c + 1))
                            own(dve.scalar_tensor_tensor(dst[:, q, 1:S], uu[:, q, c, 0:S - 1], w(0), dst[:, q, 1:S],
                                                         ALU.mult, ALU.add))
                            dve.scalar_tensor_tensor(dst[:, q, 0:S - 1], uu[:, q, c, 1:S], w(2), dst[:, q, 0:S - 1],
                                                     ALU.mult, ALU.add).then_inc(conv_done, 1)
                        dve.wait_ge(silu_done, i * 2 + (q + 1))
                        dve.wait_ge(conv_done, i * 4 + (2 * q + 2))
                        dve.tensor_tensor(gt[:, q, :], ua[:, q, :], uv[:, q, :], ALU.mult).then_inc(g_ready, 1)
                        dve.wait_ge(gH_ready, i * 2 + (q + 1))
                        at = slice(q * S, q * S + S) if first else bass.ds(i * (2 * S) + q * S, S)
                        dve.tensor_tensor(gL[:, at], gt[:, q, :], gH[:, at].bitcast(F32), ALU.subtract)\
                           .then_inc(gL_ready, 1)
                        dve.wait_ge(gL_ready, i * 2 + (q + 1))
                        at = R_CONV + 8 * (q + 2)
                        nxt = R[:, at:at + 8] if first else R[:, bass.ds(i * 16 + at, 8)]
                        own(dve.tensor_copy(cw[:, q, :], nxt))

                    own = Chain(dve, dve_ffn)
                    for q in range(2):
                        pair(0, q, True, own)
                    per = own.n
                    with dve.Fori(1, FT // 2) as i:
                        own = Chain(dve, dve_ffn, i * per)
                        for q in range(2):
                            pair(i, q, False, own)
                    for m_ in range(KT):
                        if m_ < KT - 1:
                            dve.wait_ge(wd_done, m_ + 1)
                        else:
                            dve.wait_ge(w_used, UNITS)
                        dve.tensor_tensor(x[:, m_, :], x[:, m_, :], bank[m_][:], ALU.add).then_inc(x_upd, 1)

            with nc.Block() as block:
                @block.sync
                def _(sp_):
                    for s in layer_sems:
                        sp_.sem_clear(s)

        with nc.Block() as block:
            @block.sync
            def _(sp_):
                sp_.dma_start(outT, x[:]).then_inc(out_done, 16)
                sp_.wait_ge(out_done, 16)


def constants():
    c = np.zeros((P, NC), np.float32)
    i = np.arange(P)
    c[:, C_IDENT:C_IDENT + P] = np.eye(P)
    c[:, C_MEAN_D:C_MEAN_D + P] = 1 / D
    c[:, C_MEAN_H:C_MEAN_H + P] = (i[:, None] // HD == i[None, :] // HD) / HD
    half = HD // 2
    for m in range(P):
        if m % HD < half:
            c[m + half, C_ROT + m] = -1
        else:
            c[m - half, C_ROT + m] = 1
    freq = np.float32(10000.0) ** (-np.arange(half, dtype=np.float32) / np.float32(half))
    c[:, C_FREQ] = freq[i % half]
    for l in range(DEPTH):
        lam_init = 0.8 - 0.6 * float(np.exp(-0.3 * l))
        c[:, C_LAM + l] = lam_init
        c[:, C_OML + l] = 1 - lam_init
    c[:, C_EPS] = EPS
    c[:, C_LN8] = -0.5 * np.log(HD)
    return c


def masks():
    i = np.arange(P)
    return np.concatenate([((i[:, None] // h) ^ 1) == i[None, :] // h for h in 2 ** np.arange(7)], axis=1)\
        .astype(np.int32)


def columns(w):
    d, r, n = w.shape
    return w.reshape(d, KT, P, n // P, P).transpose(0, 3, 2, 1, 4).reshape(d, n // P, P, KT * P)


def kernel(**inputs):
    import concourse.bacc as bacc
    from concourse.bass_utils import run_bass_kernel_spmd

    g = {k: np.asarray(v) for k, v in inputs.items()}
    w_in = g["w_in"]
    part = [w_in[:, :, n * 512:(n + 1) * 512] for n in range(8)]
    w_up = columns(g["w_up"]).reshape(DEPTH, 2, FT, P, UNIT).transpose(0, 2, 1, 3, 4).reshape(DEPTH, 2 * FT, P, UNIT)
    w_out = g["w_out"].reshape(DEPTH, KT, P, UNIT)[:, [hd + (4 if kind == "hg" else 0) for kind, hd in HEAD_ORDER]]
    w_down = g["w_down"].reshape(DEPTH, FT, P, UNIT)
    wts = np.concatenate([columns(part[n]) for n in (4, 5, 3, 6, 0, 1, 2, 7)] + [w_out, w_up, w_down],
                         axis=1).reshape(DEPTH * UNITS, P, UNIT)
    par = np.zeros((DEPTH, P, NR), np.float32)
    par[:, :, R_MIXG:R_MIXG + 8] = g["mix_norm_g"].reshape(DEPTH, KT, P).transpose(0, 2, 1)
    par[:, :, R_FFNG:R_FFNG + 8] = g["ffn_norm_g"].reshape(DEPTH, KT, P).transpose(0, 2, 1)
    for col, name in ((R_QG, "q_norm_g"), (R_KG, "k_norm_g"), (R_LAM, "lam_q1"), (R_LAM + 1, "lam_k1"),
                      (R_LAM + 2, "lam_q2"), (R_LAM + 3, "lam_k2")):
        par[:, :, col] = np.concatenate([g[name], g[name]], axis=1)
    par[:, :, R_DAG] = g["diff_out_g"]
    par[:, :, R_HGG] = g["hg_out_g"]
    conv = np.concatenate([g["conv_w"], g["conv_b"][:, None]], axis=1)
    conv = conv.reshape(DEPTH, 4, 2, FT, P).transpose(0, 4, 3, 2, 1)
    par[:, :, R_CONV:R_CONV + 8 * FT] = conv.reshape(DEPTH, P, 8 * FT)
    lbl = np.ascontiguousarray(g["hg_lb_logits"].reshape(DEPTH, 8, P).transpose(2, 0, 1))
    pos = np.ascontiguousarray(np.broadcast_to(g["positions"].reshape(1, S), (P, S)))
    xT = np.ascontiguousarray(g["x"].reshape(S, KT, P).transpose(2, 1, 0))
    arrays = {"xT": xT, "wts": wts, "cst": constants(), "msk": masks(), "par": par, "lbl": lbl, "pos": pos}

    nc = bacc.Bacc("TRN2", target_bir_lowering=False, num_devices=1)
    aps = {k: nc.dram_tensor(k, a.shape, mybir.dt.from_np(a.dtype), kind="ExternalInput").ap() for k, a in arrays.items()}
    out = nc.dram_tensor("outT", (P, KT, S), F32, kind="ExternalOutput").ap()
    build(nc, *[aps[k] for k in ("xT", "wts", "cst", "msk", "par", "lbl", "pos")], out)
    r = run_bass_kernel_spmd(nc, [arrays], core_ids=[0])
    y = np.asarray(r.results[0]["outT"])
    return np.ascontiguousarray(y.transpose(2, 1, 0)).reshape(1, S, D)
```

```python
from contextlib import ExitStack

import numpy as np
import concourse.bass as bass
from concourse import mybir

F32 = mybir.dt.float32
F32R = mybir.dt.float32r
I32 = mybir.dt.int32
U8 = mybir.dt.uint8
ALU = mybir.AluOpType
ACT = mybir.ActivationFunctionType
AX = mybir.AxisListType

P = 128
D = 1024
S = 512
DEPTH = 2
HEADS = 4
HD = 64
DFF = 2816
EPS = 1e-6
KT = D // P
TT = S // P
FT = DFF // P

UNIT = KT * P
N_IN, N_OUT, N_UP, N_DOWN = 32, 8, 2 * FT, FT
U_OUT = N_IN
U_UP = U_OUT + N_OUT
U_DOWN = U_UP + N_UP
UNITS = U_DOWN + N_DOWN
U_ZF, U_ZB, U_HQ, U_HI, U_DQ, U_DK, U_DV, U_HG = range(0, 32, 4)

LEVELS = 11

ITEMS = 2 * (LEVELS + 1)
STEPS = 16
HEAD_ORDER = [("hg", 0), ("hg", 1), ("da", 0), ("da", 1), ("hg", 2), ("hg", 3), ("da", 2), ("da", 3)]
AHEAD = 8


def schedule():
    order = [("unit", u) for u in range(U_HQ + 2)]
    items = iter(range(ITEMS))
    for u in range(U_HQ + 2, U_HG):
        order.append(("unit", u))
        if u == U_HQ + 2:
            order.append(("prep", 0))
        elif u == U_HQ + 2 + LEVELS + 1:
            order += [("item", next(items)), ("prep", 1)]
        else:
            order.append(("item", next(items)))
    units, posts = iter(range(U_HG, N_IN)), iter(range(8))
    for a in range(STEPS):
        if a in (0, 2, 4, 6):
            order.append(("unit", next(units)))
        post = next(posts) if 8 <= a < 15 else None
        if post is not None:
            order.append(("sum", post))
        order.append(("step", a))
        if a < 7:
            order.append(("item", next(items)))
        if post is not None:
            order.append(("post", post))
    return order + [(kind, p) for p in posts for kind in ("sum", "post")]


ORDER = schedule()

LEAD_HIGH, LEAD_LOW = 6, 2

C_IDENT = 0
C_MEAN_D = C_IDENT + P
C_MEAN_H = C_MEAN_D + P
C_ROT = C_MEAN_H + P
C_FREQ = C_ROT + P
C_LAM = C_FREQ + 1
C_OML = C_LAM + DEPTH
C_EPS = C_OML + DEPTH
C_LN8 = C_EPS + 1
NC = C_LN8 + 1

R_MIXG, R_FFNG, R_QG, R_KG, R_DAG, R_HGG = 0, 8, 16, 17, 18, 19
R_LAM = 20
R_CONV = 24
NR = R_CONV + 8 * (FT + 2)


class Chain:

    def __init__(self, eng, sem, base=0):
        self.eng, self.sem, self.base, self.n = eng, sem, base, 0

    def __call__(self, ins):
        ins.then_inc(self.sem, 1)
        self.n += 1
        self.eng.wait_ge(self.sem, self.base + self.n)


def build(nc, xT, wts, cst, msk, par, lbl, pos, outT):
    ctx = ExitStack()
    mix = ExitStack()
    ffn = ExitStack()

    def sb(name, shape, dt=F32, scope=ctx):
        return scope.enter_context(nc.sbuf_tensor(name, shape, dt))

    def sem(name):
        s = ctx.enter_context(nc.semaphore(name))
        layer_sems.append(s)
        return s

    layer_sems = []
    with ctx:
        x = sb("x", [P, KT, S])
        hH = sb("hH", [P, KT, S], F32R)
        hL = sb("hL", [P, KT, S], F32R)
        raw = sb("raw", [P, 2, UNIT])
        wH = sb("wH", [P, 2, UNIT], F32R)
        wL = sb("wL", [P, 2, UNIT], F32R)
        C = sb("C", [P, NC])
        M = sb("M", [P, 7 * P], U8)
        R = sb("R", [P, NR])
        rms = sb("rms", [P, S])
        sq = sb("sq", [P, 2, S])
        rstd = sb("rstd", [P, 2, S])
        tmp = sb("tmp", [P, 2, S])
        rotg = sb("rotg", [P, 2, P])
        lball = sb("lball", [P, DEPTH, 8])
        lb = sb("lb", [P, 8])
        omlb = sb("omlb", [P, 8])
        lamc = sb("lamc", [P, 8])
        dag = sb("dag", [P, 1])
        sm = sb("sm", [P, STEPS, 8])
        cw = sb("cw", [P, 2, 8])
        bank = [ctx.enter_context(nc.psum_tensor(f"bank{i}", [P, S], F32)) for i in range(8)]

        KK = sb("KK", [P, 2, HEADS * S], F32, mix)
        QQ = sb("QQ", [P, 2, HEADS * S], F32, mix)
        T = sb("T", [P, 2, HEADS * S], F32, mix)
        A = sb("A", [P, 2, TT, S], F32, mix)
        HI = sb("HI", [P, TT, S], F32, mix)
        V = sb("V", [P, TT, S], F32, mix)
        QK = sb("QK", [P, 8, S], F32, mix)
        E = sb("E", [P, 2, S], F32, mix)
        wT = sb("wT", [P, 2, TT, P], F32, mix)
        kx = sb("kx", [P, 2, S], F32, mix)
        ev = sb("ev", [P, 2, S], F32, mix)
        W = sb("W", [P, S], F32, mix)
        mix.close()
        gH = sb("gH", [P, FT * S], F32R, ffn)
        gL = sb("gL", [P, FT * S], F32R, ffn)
        uu = sb("uu", [P, 2, 2, S], F32, ffn)
        ua = sb("ua", [P, 2, S], F32, ffn)
        uv = sb("uv", [P, 2, S], F32, ffn)
        gt = sb("gt", [P, 2, S], F32, ffn)
        ffn.close()
        Af = A[:].rearrange("p h s t -> p (h s t)")
        sp = Af[:, 0:2 * S].rearrange("p (b t) -> p b t", b=2)
        sn = Af[:, 2 * S:4 * S].rearrange("p (b t) -> p b t", b=2)
        tt = Af[:, 4 * S:5 * S]
        ang, turns, big, wrap = (V[:, n, :] for n in range(4))
        cosT, sinT = E[:, 0, :], E[:, 1, :]
        posi = QK[:, 7, :].bitcast(I32)

        par_in = sem("par_in")
        pos_in = sem("pos_in")
        raw_in = [sem("raw_in0"), sem("raw_in1")]
        w_high = sem("w_high")
        w_split = sem("w_split")
        w_used = sem("w_used")
        gate_w = sem("gate_w")
        set_up = sem("set_up")
        lam_sum = sem("lam_sum")
        lam_exp = sem("lam_exp")
        x_upd = sem("x_upd")
        sq_ready = sem("sq_ready")
        sq_added = sem("sq_added")
        sq_mean = sem("sq_mean")
        rms_ln = sem("rms_ln")
        rms_ready = sem("rms_ready")
        hH_ready = sem("hH_ready")
        hL_ready = sem("hL_ready")
        angles = sem("angles")
        tables = sem("tables")
        unit_ev = sem("unit_ev")
        qk_sq = sem("qk_sq")
        qk_aux = sem("qk_aux")
        qk_ln = sem("qk_ln")
        qk_rstd = sem("qk_rstd")
        rope_cr = sem("rope_cr")
        rope_done = sem("rope_done")
        z_sig = sem("z_sig")
        z_done = sem("z_done")
        tok_tr = sem("tok_tr")
        tok_ev = sem("tok_ev")
        gs_done = sem("gs_done")
        hg_q = sem("hg_q")
        hg_k = sem("hg_k")
        kx_ready = sem("kx_ready")
        tot_ready = sem("tot_ready")
        lv_mm = sem("lv_mm")
        a_cp = sem("a_cp")
        a_msk = sem("a_msk")
        av_mm = sem("av_mm")
        oh_ready = sem("oh_ready")
        sc_mm = sem("sc_mm")
        neg_max = sem("neg_max")
        exps = sem("exps")
        w_ready = sem("w_ready")
        tr_mm = sem("tr_mm")
        wT_ready = sem("wT_ready")
        pv_mm = sem("pv_mm")
        od_ready = sem("od_ready")
        o_sq = sem("o_sq")
        o_sum = sem("o_sum")
        o_ln = sem("o_ln")
        o_rstd = sem("o_rstd")
        y_ready = sem("y_ready")
        yH_ready = sem("yH_ready")
        yL_ready = sem("yL_ready")
        wo_done = sem("wo_done")
        up_ev = sem("up_ev")
        conv_init = sem("conv_init")
        conv_done = sem("conv_done")
        silu_done = sem("silu_done")
        g_ready = sem("g_ready")
        gH_ready = sem("gH_ready")
        gL_ready = sem("gL_ready")
        gate_a = sem("gate_a")
        wd_done = sem("wd_done")
        dve_own = sem("dve_own")
        dve_ffn = sem("dve_ffn")
        cst_in = ctx.enter_context(nc.semaphore("cst_in"))
        bounds_in = ctx.enter_context(nc.semaphore("bounds_in"))
        masks_in = ctx.enter_context(nc.semaphore("masks_in"))
        pre_dve = ctx.enter_context(nc.semaphore("pre_dve"))
        pre_act = ctx.enter_context(nc.semaphore("pre_act"))
        x_in = [ctx.enter_context(nc.semaphore(f"x_in{k}")) for k in range(KT)]
        out_done = ctx.enter_context(nc.semaphore("out_done"))

        def cst_at(c, n=P):
            return C[:, c:c + n]

        def blocks(v, h):
            return v.rearrange("p (n two h) -> p n two h", two=2, h=h)

        def head(t, plane, hd, i=0, n=TT):
            return t[:, plane, hd * S + i * P:hd * S + (i + n) * P]

        def diag(r):
            return bass.AP(tensor=A[:].tensor, offset=r * TT * S, ap=[[2 * TT * S, P], [S + P, TT], [1, P]])

        def gs(hd):
            return T[:, hd // 2, (hd % 2) * 2 * S + S:(hd % 2) * 2 * S + 2 * S]

        def totals(pair, h):
            if h == 1:
                return T[:, :, pair * 2 * S:(pair + 1) * 2 * S]
            if h == 2:
                return wT[:].rearrange("p a k q -> p a (k q)")
            at = pair * 2 * S + S - 4 * S // h
            return T[:, :, at:at + 2 * S // h]

        def token_head(u):
            if U_HI < u <= U_DQ:
                return u - 1 - U_HI
            if U_DV < u <= U_HG:
                return u - 1 - U_DV + 4
            return None

        def unit_bank(u):
            return bank[4 if u == 0 else u % 2]

        def score_bank(a, c):
            return bank[(2 if a > AHEAD and a % 2 else 4) + c]

        def scores_after(n):
            return [a for a in ((n + 1,) if n < AHEAD else (n + 1, n + 2) if n == AHEAD else (n + 2,)) if a < STEPS]

        def crossing(t, hd, i, h, left, n=1):
            side = HEADS * S * (1 if left == 0 else -1)
            return bass.AP(tensor=t[:].tensor, offset=left * HEADS * S + hd * S + i * P,
                           ap=[[2 * HEADS * S, P], [2 * h, n * P // (2 * h)], [side + h, 2], [1, h]])

        def out_head(p):
            kind, hd = HEAD_ORDER[p]
            return head(QQ, 0, hd) if kind == "hg" else QK[:, hd, :]

        def input_high(act, k):
            act.activation(hH[:, k, :], x[:, k, :], ACT.Identity, scale=R[:, R_MIXG + k:R_MIXG + k + 1])\
               .then_inc(hH_ready, 1)

        def low(dve, k, n, col):
            dve.wait_ge(hH_ready, 8 * n + k + 1)
            dve.scalar_tensor_tensor(hL[:, k, :], x[:, k, :], R[:, col + k:col + k + 1], hH[:, k, :].bitcast(F32),
                                     ALU.mult, ALU.subtract).then_inc(hL_ready, 1)

        def square_of(k):
            return rstd[:, 0, :] if k == 0 else (sq, tmp)[(k - 1) // 2 % 2][:, (k - 1) % 2, :]

        def add_square(eng, k, n):
            eng.wait_ge(sq_ready, 8 * n + k + 1)
            if k + n > 1:
                eng.wait_ge(sq_added, 7 * n + k - 1)
            eng.tensor_tensor(square_of(0), square_of(0), square_of(k), ALU.add).then_inc(sq_added, 1)

        def load_params(sp_, row):
            sp_.dma_start(R[:], par[row].rearrange("a p n -> (a p) n")).then_inc(par_in, 16)

        lraw, le, lp = sm[:, 0:2, :], sm[:, 2:4, :], sm[:, 4:6, :]
        lmax, lsum = sm[:, 6, :], sm[:, 7, :]
        with nc.Block() as block:
            @block.sync
            def _(sp_):
                load_params(sp_, slice(0, 1))
                for k in range(KT):
                    sp_.dma_start(x[:, k, :], xT[:, k, :]).then_inc(x_in[k], 16)
                sp_.dma_start(raw[:, 1, :], wts[1]).then_inc(raw_in[1], 16)
                sp_.dma_start(M[:].bitcast(I32), msk).then_inc(masks_in, 16)
                sp_.sem_inc(out_done, 16 * KT)
                sp_.wait_ge(cst_in, 16)

            @block.gpsimd
            def _(pool):
                pool.wait_ge(w_high, 1)
                pool.tensor_tensor(wL[:, 0, :], raw[:, 0, :], wH[:, 0, :].bitcast(F32), ALU.subtract).then_inc(w_split, 1)

            @block.vector
            def _(dve):
                ch = Chain(dve, pre_dve)
                dve.wait_ge(bounds_in, 16)
                ch(dve.tensor_copy(lmax, lraw[:, 0, :]))
                for l in range(1, DEPTH):
                    ch(dve.tensor_tensor(lmax, lmax, lraw[:, l, :], ALU.max))
                for l in range(DEPTH):
                    ch(dve.tensor_tensor(le[:, l, :], lraw[:, l, :], lmax, ALU.subtract))
                dve.wait_ge(pre_act, 1)
                ch(dve.tensor_copy(lsum, le[:, 0, :]))
                for l in range(1, DEPTH):
                    ch(dve.tensor_tensor(lsum, lsum, le[:, l, :], ALU.add))
                ch(dve.reciprocal(lsum, lsum))
                for l in range(DEPTH):
                    ch(dve.tensor_tensor(lp[:, l, :], le[:, l, :], lsum, ALU.mult))
                ch(dve.tensor_copy(lmax, lp[:, 0, :]))
                for l in range(DEPTH):
                    if l:
                        ch(dve.tensor_tensor(lmax, lmax, lp[:, l, :], ALU.add))
                    ch(dve.tensor_tensor(lball[:, l, :], lmax, lp[:, 0, :], ALU.subtract))
                    ch(dve.tensor_scalar(lball[:, l, :], lball[:, l, :], 0.0, 1.0 - 1e-4, ALU.max, ALU.min))
                for k in range(LEAD_LOW):
                    low(dve, k, 0, R_MIXG)

            @block.scalar
            def _(act):
                act.dma_start(lraw, lbl).then_inc(bounds_in, 16)
                act.dma_start(raw[:, 0, :], wts[0]).then_inc(raw_in[0], 16)
                act.dma_start(C[:], cst).then_inc(cst_in, 16)
                act.wait_ge(pre_dve, 2 * DEPTH)
                act.activation(le, le, ACT.Exp).then_inc(pre_act, 1)
                act.wait_ge(raw_in[0], 16)
                act.activation(wH[:, 0, :], raw[:, 0, :], ACT.Copy).then_inc(w_high, 1)
                act.wait_ge(par_in, 16)
                for k in range(LEAD_HIGH):
                    act.wait_ge(x_in[k], 16)
                    input_high(act, k)

        with nc.Fori(0, DEPTH) as layer:
            with nc.Block() as block:
                @block.sync
                def _(sp_):
                    def load(s, row):
                        sp_.dma_start(raw[:, s, :], wts[bass.ds(row, 1)].rearrange("a p n -> (a p) n"))\
                           .then_inc(raw_in[s], 16)

                    sp_.wait_ge(out_done, 16 * KT)
                    sp_.sem_clear(out_done)
                    sp_.dma_start(posi, pos).then_inc(pos_in, 16)
                    with sp_.Fori(1, UNITS // 2 + 1) as j:
                        for s in range(2):
                            row = layer * UNITS + j * 2 + s
                            sp_.wait_ge(w_split, j * 2 + s - 1)
                            load(s, row)
                    sp_.wait_ge(dve_ffn, 3 * FT)
                    load_params(sp_, bass.ds(layer + 1, 1))
                    for s in range(2):
                        sp_.wait_ge(raw_in[s], 16 * (UNITS // 2 + 1))
                    sp_.wait_ge(par_in, 32)
                    for m_ in range(KT):
                        sp_.wait_ge(x_upd, KT + m_ + 1)
                        sp_.dma_start(outT[:, m_, :], x[:, m_, :]).then_inc(out_done, 16)

                @block.gpsimd
                def _(pool):
                    def split(u, s):
                        pool.wait_ge(w_high, u + 1)
                        pool.tensor_tensor(wL[:, s, :], raw[:, s, :], wH[:, s, :].bitcast(F32), ALU.subtract)\
                            .then_inc(w_split, 1)

                    def split_now(u):
                        if u < UNITS:
                            split(u, u % 2)

                    def grow(pair, lv):
                        h = 2 ** (lv - 1)
                        tot = totals(pair, h)
                        pool.wait_ge(lv_mm, 22 * pair + 2 * lv + 2)
                        pool.wait_ge(hg_q, 10 * pair + lv + 1)
                        if pair + lv > 1:
                            pool.wait_ge(hg_k, 8 * pair + lv - 1)
                        if lv == 2:
                            pool.wait_ge(tot_ready, 7 * pair + 1)
                        if 1 < h < 128:
                            for d in range(2):
                                w = tot[:, d, :].rearrange("p (n two) -> p n two", two=2)
                                nxt = pool.tensor_tensor(totals(pair, 2 * h)[:, d, :], w[:, :, 0], w[:, :, 1], ALU.mult)
                            nxt.then_inc(tot_ready, 1)
                        n = S // h
                        for half in range(2):
                            v = blocks(KK[:, half, pair * 2 * S:(pair + 1) * 2 * S], h)[:, :, half, :]
                            w = tot[:, half, :].rearrange("p (n two o) -> p n two o", two=2, o=1)[:, :, 1 - half, :]
                            last = pool.tensor_tensor(v, v, w.to_broadcast([P, n, h]), ALU.mult)
                        last.then_inc(hg_k, 1)

                    def square(p):
                        kind, hd = HEAD_ORDER[p]
                        pool.wait_ge(*((oh_ready, hd + 1) if kind == "hg" else (od_ready, hd + 1)))
                        if p >= 2:
                            pool.wait_ge(o_sum, p - 1)
                        pool.tensor_tensor(sq[:, p % 2, :], out_head(p), out_head(p), ALU.mult).then_inc(o_sq, 1)

                    def post(p):
                        t = tmp[:, p % 2, :]
                        pool.wait_ge(y_ready, p + 1)
                        pool.tensor_scalar(hH[:, p, :], t, 1.0, 1.0, ALU.mult, ALU.mult).then_inc(yH_ready, 1)
                        pool.wait_ge(yH_ready, p + 1)
                        pool.tensor_tensor(hL[:, p, :], t, hH[:, p, :].bitcast(F32), ALU.subtract).then_inc(yL_ready, 1)

                    for kind, n in ORDER:
                        if kind == "unit":
                            if n == 0:
                                split_now(1)
                            split_now(n + 2)
                        elif kind == "item":
                            pair, lv = divmod(n, LEVELS + 1)
                            if 1 <= lv <= 8:
                                grow(pair, lv)
                            if n == ITEMS - 1:
                                square(0)
                                square(1)
                        elif kind == "post":
                            post(n)
                            if n + 2 < 7:
                                square(n + 2)
                    with pool.Fori(N_IN // 2 + 1, U_UP // 2) as j:
                        for s in range(2):
                            split(j * 2 + s, s)
                    split(U_UP, 0)
                    for k in range(1, KT):
                        add_square(pool, k, 1)
                        if k == 3:
                            split(U_UP + 1, 1)
                    with pool.Fori(U_UP // 2 + 1, UNITS // 2) as j:
                        for s in range(2):
                            split(j * 2 + s, s)
                    split(UNITS, 0)

                @block.tensor
                def _(pe):
                    def triple(out, s, a, rhs_h, rhs_l, first, last):
                        pe.matmul(out, wH[:, s, a:a + P], rhs_h, start=first, stop=False)
                        pe.matmul(out, wL[:, s, a:a + P], rhs_h, start=False, stop=False)
                        return pe.matmul(out, wH[:, s, a:a + P], rhs_l, start=False, stop=last)

                    def column(u, out, fresh=None, mean=None):
                        pe.wait_ge(w_split, u + 1)
                        for k in range(KT):
                            if fresh is not None:
                                pe.wait_ge(hL_ready, 8 * fresh + k + 1)
                            if mean is not None and k == (0 if mean else 5):
                                pe.wait_ge(sq_added, 7 * mean + 7)
                                pe.matmul(bank[5][:], cst_at(C_MEAN_D), square_of(0), start=True, stop=True)\
                                  .then_inc(sq_mean, 1)
                            m = triple(out, u % 2, k * P, hH[:, k, :], hL[:, k, :], k == 0, k == KT - 1)
                        m.then_inc(w_used, 1)

                    def unit(u):
                        if u > 2:
                            pe.wait_ge(unit_ev, u - 1)
                        column(u, unit_bank(u)[:], 0 if u == 0 else None, 0 if u == 1 else None)
                        if U_DQ < u <= U_DV:
                            aux(u - 1 - U_DQ)
                        if token_head(u) is not None:
                            to_tokens(token_head(u))

                    def aux(n):
                        pe.wait_ge(qk_sq, n + 1)
                        if n:
                            pe.wait_ge(qk_ln, n)
                            pe.wait_ge(rope_cr, n)
                        else:
                            pe.wait_ge(set_up, 2)
                            pe.wait_ge(tok_ev, 4)
                        pe.matmul(bank[6][:], cst_at(C_MEAN_H), sq[:, n % 2, :], start=True, stop=True)
                        pe.matmul(bank[7][:], rotg[:, n // 4, :], QK[:, n, :], start=True, stop=True).then_inc(qk_aux, 1)

                    def to_tokens(n):
                        pe.wait_ge(unit_ev, (U_HI if n < 4 else U_DV - 4) + n + 1)
                        if n == 4:
                            pe.wait_ge(qk_ln, 8)
                            pe.wait_ge(rope_cr, 8)
                        if n >= 2:
                            pe.wait_ge(tok_ev, n - 1)
                        for i in range(TT):
                            m = pe.transpose(bank[6 + n % 2][:, i * P:i * P + P], ev[:, n % 2, i * P:i * P + P],
                                             cst_at(C_IDENT))
                        m.then_inc(tok_tr, 1)

                    def item(n):
                        pair, lv = divmod(n, LEVELS + 1)
                        if lv == LEVELS:
                            pe.wait_ge(tok_ev, 4)
                            for r in range(2):
                                hd = 2 * pair + r
                                pe.wait_ge(a_cp, 8 * pair + 6 + r + 1)
                                for i in range(TT):
                                    m = pe.matmul(bank[2 + r][:], HI[:, i, hd * P:hd * P + P], A[:, r, i, :],
                                                  start=i == 0, stop=i == TT - 1)
                                m.then_inc(av_mm, 1)
                            return
                        pe.wait_ge(hg_q, 10 * pair + min(lv, 9) + 1)
                        if 1 <= lv <= 7:
                            pe.wait_ge(kx_ready, 7 * pair + lv)
                        elif lv:
                            pe.wait_ge(hg_k, 8 * pair + min(lv, 9) - 1)
                        for r in range(2):
                            hd, b = 2 * pair + r, bank[2 + r]
                            if lv == 0:
                                if pair:
                                    pe.wait_ge(oh_ready, r + 1)
                            elif lv == 1 or lv > 8:
                                pe.wait_ge(a_cp, 8 * pair + (0 if lv == 1 else 2 * (lv - 8)) + r + 1)
                            else:
                                pe.wait_ge(a_msk, 14 * pair + 2 * (lv - 2) + r + 1)
                            if lv <= 8:
                                for i in range(TT):
                                    o = b[:, i * P:i * P + P]
                                    if lv == 0:
                                        m = pe.matmul(o, kx[:, r, i * P:i * P + P], head(QQ, 1, hd, i, 1),
                                                      start=True, stop=True)
                                    elif lv < 8:
                                        h = 2 ** (lv - 1)
                                        m = pe.matmul(o.rearrange("p (n two h) -> p n two h", two=2, h=h),
                                                      kx[:, r, i * P:i * P + P], crossing(QQ, hd, i, h, 0),
                                                      start=True, stop=True)
                                    else:
                                        m = pe.matmul(o, head(KK, i % 2, hd, i, 1), head(QQ, 1 - i % 2, hd, i ^ 1, 1),
                                                      start=True, stop=True)
                            else:
                                half = lv - 9
                                for i in range(2):
                                    m = pe.matmul(b[:, i * 2 * P:(i + 1) * 2 * P], head(KK, half, hd, 2 * half + i, 1),
                                                  head(QQ, 1 - half, hd, 2 - 2 * half, 2), start=True, stop=True)
                            m.then_inc(lv_mm, 1)

                    def scores(a):
                        hd, qt = divmod(a, 4)
                        if a == 0:
                            pe.wait_ge(rope_done, 8)
                            pe.wait_ge(rms_ln, 1)
                        elif a <= AHEAD:
                            pe.wait_ge(exps, a)
                        elif a == AHEAD + 1:
                            pe.wait_ge(oh_ready, 4)
                        else:
                            pe.wait_ge(exps, a - 1)
                        for c in range(2):
                            r = slice(HD * c, HD * c + HD)
                            m = pe.matmul(score_bank(a, c)[:], QK[r, hd, qt * P:qt * P + P], QK[r, 4 + hd, :],
                                          start=True, stop=True)
                        m.then_inc(sc_mm, 1)

                    def turn(a):
                        if a == 0:
                            pe.wait_ge(tok_ev, 7)
                        else:
                            pe.wait_ge(wT_ready, a)
                        pe.wait_ge(w_ready, a + 1)
                        for k in range(TT):
                            m = pe.transpose(bank[6][:, k * P:k * P + P], W[:, k * P:k * P + P], cst_at(C_IDENT))
                        m.then_inc(tr_mm, 1)

                    def values(a):
                        hd, qt = divmod(a, 4)
                        pe.wait_ge(wT_ready, a + 1)
                        if a == 0:
                            pe.wait_ge(tok_ev, 8)
                        elif qt == 0:
                            pe.wait_ge(od_ready, hd)
                        for k in range(TT):
                            m = pe.matmul(bank[7][:, qt * P:qt * P + P], V[:, k, hd * P:hd * P + P], wT[:, a % 2, k, :],
                                          start=k == 0, stop=k == TT - 1)
                        m.then_inc(pv_mm, 1)

                    def post(p):
                        pe.wait_ge(o_sq, p + 1)
                        if p:
                            pe.wait_ge(o_ln, p)
                        else:
                            pe.wait_ge(unit_ev, N_IN)
                        pe.matmul(bank[1][:], cst_at(C_MEAN_D), sq[:, p % 2, :], start=True, stop=True).then_inc(o_sum, 1)

                    def out_tile(p, m_):
                        return triple(bank[m_][:], (U_OUT + p) % 2, m_ * P, hH[:, p, :], hL[:, p, :], p == 0, p == KT - 1)

                    pe.wait_ge(set_up, 1)
                    pe.matmul(bank[3][:, 0:2], cst_at(C_MEAN_D), lamc[:, 0:2], start=True, stop=True).then_inc(lam_sum, 1)
                    for kind, n in ORDER:
                        if kind == "unit":
                            unit(n)
                            if n == U_HG - 1:
                                scores(0)
                        elif kind == "item":
                            if n == 0:
                                pe.wait_ge(lam_exp, 1)
                            item(n)
                        elif kind == "step":
                            for a in scores_after(n):
                                scores(a)
                            if n == STEPS - 1:
                                pe.wait_ge(exps, STEPS - 1)
                                out_tile(0, 4)
                                out_tile(0, 5)
                            if n:
                                values(n - 1)
                            if n == STEPS - 2:
                                pe.wait_ge(w_split, U_OUT + 1)
                                pe.wait_ge(yL_ready, 1)
                                out_tile(0, 0)
                            turn(n)
                        elif kind == "sum":
                            if n < KT - 1:
                                post(n)
                            else:
                                pe.wait_ge(exps, STEPS)
                                out_tile(0, 2)
                                out_tile(0, 3)
                                values(STEPS - 1)

                    pe.wait_ge(wT_ready, STEPS)
                    out_tile(0, 6)
                    post(KT - 1)
                    pe.wait_ge(od_ready, 4)
                    out_tile(0, 7)
                    pe.wait_ge(w_split, U_OUT + 2)
                    pe.wait_ge(yL_ready, 2)
                    out_tile(1, 0)
                    pe.wait_ge(o_ln, 8)
                    out_tile(0, 1).then_inc(w_used, 1)
                    for m_ in range(2, KT):
                        out_tile(1, m_)
                    out_tile(1, 1).then_inc(w_used, 1)
                    for p in range(2, KT):
                        pe.wait_ge(w_split, U_OUT + p + 1)
                        pe.wait_ge(yL_ready, p + 1)
                        for m_ in range(KT):
                            m = out_tile(p, m_)
                            if p == KT - 1 and m_ < KT - 1:
                                m.then_inc(wo_done, 1)
                        m.then_inc(w_used, 1)

                    pe.wait_ge(x_upd, 1)

                    def pair(i, q, first):
                        for c in range(2):
                            b = bank[2 * q + c]
                            if first:
                                if q == 0 and c == 1:
                                    pe.wait_ge(x_upd, 2)
                                if q == 1:
                                    pe.wait_ge(x_upd, 8)
                                column(U_UP + 2 * q + c, b[:], 1 if q + c == 0 else None, 1 if (q, c) == (1, 0) else None)
                                continue
                            pe.wait_ge(w_split, i * 4 + (U_UP + 2 * q + c + 1))
                            pe.wait_ge(up_ev, i * 4 + (2 * (q - 2) + c + 1))
                            for k in range(KT):
                                m = triple(b[:], c, k * P, hH[:, k, :], hL[:, k, :], k == 0, k == KT - 1)
                            m.then_inc(w_used, 1)

                    for q in range(2):
                        pair(0, q, True)
                    with pe.Fori(1, FT // 2) as i:
                        for q in range(2):
                            pair(i, q, False)

                    def down(k, s, gh, gl, first, last):
                        pe.wait_ge(w_split, k + (U_DOWN + 1))
                        pe.wait_ge(gL_ready, k + 1)
                        for n in range(KT):
                            m_ = n if last else (n + 4) % KT
                            if first and m_ == 0:
                                pe.wait_ge(up_ev, 2 * FT)
                            m = triple(bank[m_][:], s, m_ * P, gh, gl, first, last)
                            if last and m_ < KT - 1:
                                m.then_inc(wd_done, 1)
                        m.then_inc(w_used, 1)

                    for k in range(2):
                        down(k, k, gH[:, k * S:(k + 1) * S], gL[:, k * S:(k + 1) * S], k == 0, False)
                    with pe.Fori(1, FT // 2 - 1) as i:
                        for s in range(2):
                            down(i * 2 + s, s, gH[:, bass.ds(i * (2 * S) + s * S, S)],
                                 gL[:, bass.ds(i * (2 * S) + s * S, S)], False, False)
                    for k in range(FT - 2, FT):
                        down(k, k % 2, gH[:, k * S:(k + 1) * S], gL[:, k * S:(k + 1) * S], False, k == FT - 1)

                @block.scalar
                def _(act):
                    eps = cst_at(C_EPS, 1)

                    def high(u, s, turn, first=False, looped=False):
                        act.wait_ge(raw_in[s], turn)
                        if not first:
                            act.wait_ge(w_used, u - 1)
                        if looped:
                            act.sem_inc(gate_w, 1)
                        act.activation(wH[:, s, :], raw[:, s, :], ACT.Copy).then_inc(w_high, 1)

                    def high_now(u):
                        high(u, u % 2, 16 * (u // 2 + 1), u < 2)

                    def square(n, k):
                        if k > 4:
                            act.wait_ge(sq_added, 7 * n + k - 4)
                        act.activation(square_of(k), x[:, k, :], ACT.Square).then_inc(sq_ready, 1)

                    def root(n):
                        act.wait_ge(sq_mean, n + 1)
                        act.activation(rms[:], bank[5][:], ACT.Ln, bias=eps).then_inc(rms_ln, 1)
                        act.wait_ge(rms_ln, n + 1)
                        act.activation(rms[:], rms[:], ACT.Exp, scale=-0.5).then_inc(rms_ready, 1)

                    def logs():
                        nc.scalar.preload_act_table_set("natural_log_exp_and_others")

                    logs()
                    high_now(1)
                    for k in range(LEAD_HIGH, KT):
                        act.wait_ge(x_in[k], 16)
                        input_high(act, k)
                    for k in range(KT):
                        square(0, k)
                    high_now(2)
                    root(0)
                    act.wait_ge(lam_sum, 1)
                    act.activation(lamc[:, 2:4], bank[3][:, 0:2], ACT.Exp, scale=0.5 * D).then_inc(lam_exp, 1)

                    def rope_stats(n):
                        act.wait_ge(qk_aux, n + 1)
                        if n >= 2:
                            act.wait_ge(rope_done, n - 1)
                        r = rstd[:, n % 2, :]
                        act.activation(r, bank[6][:], ACT.Ln, bias=eps).then_inc(qk_ln, 1)
                        act.wait_ge(qk_ln, n + 1)
                        act.activation(r, r, ACT.Exp, scale=-0.5,
                                       bias=cst_at(C_LN8, 1) if n < 4 else 0.0).then_inc(qk_rstd, 1)

                    def tokens(n):
                        act.wait_ge(tok_tr, n + 1)
                        dst = HI if n < 4 else V
                        act.activation(dst[:, :, (n % 4) * P:(n % 4 + 1) * P],
                                       bank[6 + n % 2][:].rearrange("p (i c) -> p i c", i=TT), ACT.Copy)\
                            .then_inc(tok_ev, 1)

                    def unit(u):
                        if u:
                            high_now(u + 2)
                        if U_DQ < u <= U_DV:
                            rope_stats(u - 1 - U_DQ)
                        if token_head(u) is not None:
                            tokens(token_head(u))
                        if u < U_HQ:
                            act.wait_ge(unit_ev, u + 1)
                            if u >= U_ZF + 2:
                                act.wait_ge(z_done, u - U_ZF - 1)
                            act.activation(sp[:, u % 2, :], ev[:, u % 2, :], ACT.Sigmoid)
                            act.activation(sn[:, u % 2, :], ev[:, u % 2, :], ACT.Sigmoid, scale=-1.0).then_inc(z_sig, 1)
                        elif u == U_HI + 1:
                            act.wait_ge(angles, 1)
                            act.activation(cosT, turns, ACT.Sin)
                            act.activation(sinT, ang, ACT.Sin).then_inc(tables, 1)
                            logs()
                        elif U_DQ <= u < U_DV:
                            n = u - U_DQ
                            act.wait_ge(unit_ev, u + 1)
                            if n >= 2:
                                act.wait_ge(qk_aux, n - 1)
                            act.activation(sq[:, n % 2, :], QK[:, n, :], ACT.Square).then_inc(qk_sq, 1)
                        elif u == N_IN - 1:
                            for hd in range(HEADS):
                                act.wait_ge(unit_ev, U_HG + hd + 1)
                                act.activation(gs(hd), gs(hd), ACT.Silu).then_inc(gs_done, 1)
                            logs()

                    def item(n):
                        pair, lv = divmod(n, LEVELS + 1)
                        for r in range(2):
                            if lv == LEVELS:
                                act.wait_ge(av_mm, 2 * pair + r + 1)
                                act.activation(head(QQ, 0, 2 * pair + r), bank[2 + r][:], ACT.Copy).then_inc(oh_ready, 1)
                                continue
                            if 1 <= lv <= 7:
                                continue
                            act.wait_ge(lv_mm, 22 * pair + 2 * lv + r + 1)
                            b = bank[2 + r][:].rearrange("p (i t) -> p i t", i=TT)
                            if lv == 0:
                                if pair:
                                    act.wait_ge(av_mm, r + 1)
                                act.activation(diag(r), b, ACT.Copy).then_inc(a_cp, 1)
                            elif lv == 8:
                                base, row = r * TT * S, 2 * TT * S
                                for o in range(2):
                                    dst = bass.AP(tensor=A[:].tensor, offset=base + (P if o == 0 else S),
                                                  ap=[[row, P], [2 * S + 2 * P, 2], [1, P]])
                                    cp = act.activation(dst, b[:, o::2, :], ACT.Copy)
                                cp.then_inc(a_cp, 1)
                            else:
                                half = lv - 9
                                act.activation(A[:, r, 2 * half:2 * half + 2, (2 - 2 * half) * P:(4 - 2 * half) * P],
                                               bank[2 + r][:].rearrange("p (i t) -> p i t", i=2), ACT.Copy)\
                                    .then_inc(a_cp, 1)

                        if lv <= 6:
                            act.wait_ge(lv_mm, 22 * pair + 2 * lv + 2)
                            if lv:
                                act.wait_ge(hg_k, 8 * pair + lv)
                            h = 2 ** lv
                            act.activation(kx[:].rearrange("p r t -> p (r t)").rearrange("p (n two h) -> p n two h", two=2, h=h),
                                           crossing(KK, 2 * pair, 0, h, 0, 2 * TT), ACT.Copy).then_inc(kx_ready, 1)

                    def back(a):
                        act.wait_ge(tr_mm, a + 1)
                        if a == 0:
                            act.wait_ge(hg_q, 10 + 4)
                            act.wait_ge(hg_k, 8 + 2)
                            act.wait_ge(tot_ready, 7 + 2)
                        if a >= 2:
                            act.wait_ge(pv_mm, a - 1)
                        act.activation(wT[:, a % 2, :, :], bank[6][:].rearrange("p (k q) -> p k q", k=TT), ACT.Copy)\
                            .then_inc(wT_ready, 1)

                    def exponentials(a):
                        act.wait_ge(neg_max, a + 1)
                        if a == 0:
                            act.wait_ge(rope_cr, 8)
                        else:
                            act.wait_ge(w_ready, a)
                        for c in range(2):
                            e = act.activation(E[:, c, :], score_bank(a, c)[:], ACT.Exp,
                                               bias=sm[:, a, c:c + 1], accum_out=sm[:, a, 2 + c:3 + c])
                        e.then_inc(exps, 1)

                    def head_out(hd):
                        act.wait_ge(pv_mm, 4 * hd + 4)
                        act.activation(QK[:, hd, :], bank[7][:], ACT.Copy).then_inc(od_ready, 1)

                    def post(p):
                        act.wait_ge(o_sum, p + 1)
                        if p >= 2:
                            act.wait_ge(y_ready, p - 1)
                        r = rstd[:, p % 2, :]
                        act.activation(r, bank[1][:], ACT.Ln, bias=eps, scale=float(D // P)).then_inc(o_ln, 1)
                        act.wait_ge(o_ln, p + 1)
                        act.activation(r, r, ACT.Exp, scale=-0.5).then_inc(o_rstd, 1)

                    for kind, n in ORDER:
                        if kind == "unit":
                            unit(n)
                            if n == U_HG - 1:
                                exponentials(0)
                        elif kind == "item":
                            item(n)
                        elif kind == "step":
                            if n and n % 4 == 0:
                                head_out(n // 4 - 1)
                            if n < AHEAD:
                                back(n)
                            if n + 1 < STEPS:
                                exponentials(n + 1)
                            if n >= AHEAD:
                                back(n)
                        elif kind == "sum":
                            if n == KT - 1:
                                act.wait_ge(pv_mm, STEPS)
                                act.wait_ge(o_sum, n - 1)
                                act.activation(sq[:, n % 2, :], bank[7][:], ACT.Square).then_inc(o_sq, 1)
                                head_out(3)
                            post(n)

                    for u in range(U_OUT, U_UP - 1):
                        high_now(u + 2)
                    for k in range(KT):
                        act.wait_ge(x_upd, k + 1)
                        if k == KT - 1:
                            act.wait_ge(w_used, U_UP)
                        act.activation(hH[:, k, :], x[:, k, :], ACT.Identity,
                                       scale=R[:, R_FFNG + k:R_FFNG + k + 1]).then_inc(hH_ready, 1)
                        square(1, k)
                        if k == 4:
                            high_now(U_UP + 1)
                    high_now(U_UP + 2)
                    root(1)
                    high_now(U_UP + 3)

                    def pair(i, q, first):
                        for c, dst in enumerate((ua, uv)):
                            u = U_UP + 2 * q + c + 2
                            if not first:
                                high(i * 4 + u, c, i * 32 + 16 * (u // 2 + 1), looped=True)
                                act.wait_ge(g_ready, i * 2 + (q - 1))
                            act.wait_ge(up_ev, i * 4 + (2 * q + c + 1))
                            act.activation(dst[:, q, :], uu[:, q, c, :], ACT.Identity, bias=cw[:, q, 4 * c + 3:4 * c + 4],
                                           scale=cw[:, q, 4 * c + 1:4 * c + 2]).then_inc(conv_init, 1)
                        if first:
                            high_now(U_UP + 4 + q)
                        act.wait_ge(conv_done, i * 4 + (2 * q + 1))
                        act.activation(ua[:, q, :], ua[:, q, :], ACT.Silu).then_inc(silu_done, 1)
                        act.wait_ge(g_ready, i * 2 + (q + 1))
                        act.sem_inc(gate_a, 1)
                        cols = gH[:, q * S:q * S + S] if first else gH[:, bass.ds(i * (2 * S) + q * S, S)]
                        act.activation(cols, gt[:, q, :], ACT.Copy).then_inc(gH_ready, 1)

                    for q in range(2):
                        pair(0, q, True)
                    with act.Fori(1, FT // 2) as i:
                        for q in range(2):
                            pair(i, q, False)
                    with act.Fori(U_DOWN // 2 + 1, UNITS // 2) as j:
                        for s in range(2):
                            high(j * 2 + s, s, j * 16 + 16, looped=True)
                    high_now(UNITS)
                    act.wait_ge(par_in, 32)
                    for k in range(LEAD_HIGH):
                        act.wait_ge(x_upd, KT + k + 1)
                        input_high(act, k)

                @block.vector
                def _(dve):
                    ch = Chain(dve, dve_own)

                    lv4 = R[:, R_LAM:R_LAM + 4].rearrange("p (a b) -> p a b", b=2)
                    dve.tensor_tensor(lamc[:, 0:2], lv4[:, :, 0], lv4[:, :, 1], ALU.mult).then_inc(set_up, 1)
                    for k in range(LEAD_LOW, KT):
                        low(dve, k, 0, R_MIXG)
                    for k in range(1, KT):
                        add_square(dve, k, 0)
                    ch(dve.tensor_copy(lb[:], lball[:].rearrange("p l c -> p (l c)")[:, bass.ds(layer * 8, 8)]))
                    ch(dve.tensor_scalar(omlb[:], lb[:], -1.0, 1.0, ALU.mult, ALU.add))
                    ch(dve.tensor_copy(lamc[:, 4:5], C[:, bass.ds(layer + C_LAM, 1)]))
                    ch(dve.tensor_copy(lamc[:, 5:6], C[:, bass.ds(layer + C_OML, 1)]))
                    ch(dve.tensor_tensor(dag[:], R[:, R_DAG:R_DAG + 1], lamc[:, 5:6], ALU.mult))
                    for c in range(2):
                        m = dve.tensor_scalar(rotg[:, c, :], cst_at(C_ROT), R[:, R_QG + c:R_QG + c + 1], None, ALU.mult)
                    m.then_inc(set_up, 1)

                    def rotary(part):
                        TWO_PI = 2 * np.pi
                        c1 = float(np.floor(TWO_PI * 2 ** 9) / 2 ** 9)
                        c2 = float(np.floor((TWO_PI - c1) * 2 ** 21) / 2 ** 21)
                        c3 = float(np.float32(TWO_PI - c1 - c2))
                        BIG = float(1.5 * 2 ** 23)
                        PI = float(np.nextafter(np.float32(np.pi), np.float32(0)))
                        if part == 0:
                            dve.wait_ge(pos_in, 16)
                            ch(dve.tensor_copy(turns, posi))
                            ch(dve.tensor_scalar(ang, turns, C[:, C_FREQ:C_FREQ + 1], None, ALU.mult))
                            ch(dve.tensor_scalar(turns, ang, float(1 / TWO_PI), BIG, ALU.mult, ALU.add))
                            ch(dve.tensor_scalar(turns, turns, -BIG, None, ALU.add))
                            ch(dve.tensor_scalar(big, turns, 1 / 2048, BIG, ALU.mult, ALU.add))
                            ch(dve.tensor_scalar(big, big, -BIG, 2048.0, ALU.add, ALU.mult))
                            ch(dve.tensor_tensor(turns, turns, big, ALU.subtract))
                        elif part == 1:
                            for c in (c1, c2, c3):
                                ch(dve.scalar_tensor_tensor(ang, big, -c, ang, ALU.mult, ALU.add))
                                ch(dve.scalar_tensor_tensor(ang, turns, -c, ang, ALU.mult, ALU.add))
                        else:
                            ch(dve.tensor_scalar(turns, ang, float(np.pi / 2), None, ALU.add))
                            ch(dve.tensor_scalar(wrap, turns, float(np.pi), -TWO_PI, ALU.is_gt, ALU.mult))
                            ch(dve.tensor_tensor(turns, turns, wrap, ALU.add))
                            ch(dve.tensor_scalar(turns, turns, PI, -PI, ALU.min, ALU.max))
                            dve.tensor_scalar(ang, ang, PI, -PI, ALU.min, ALU.max).then_inc(angles, 1)

                    dve.wait_ge(lam_exp, 1)
                    ch(dve.tensor_tensor(lamc[:, 6:7], lamc[:, 3:4], lamc[:, 2:3], ALU.subtract))
                    ch(dve.tensor_tensor(lamc[:, 7:8], lamc[:, 6:7], lamc[:, 4:5], ALU.subtract))
                    e30 = float(np.exp(30.0))

                    def evict(u):
                        dve.wait_ge(w_used, u + 1)
                        if U_DQ <= u < U_DV:
                            dst = QK[:, u - U_DQ, :]
                        elif U_HQ <= u < U_HI:
                            dst = head(QQ, 1, u - U_HQ)
                        elif u >= U_HG:
                            dst = gs(u - U_HG)
                            dve.wait_ge(hg_q, 10 + 3)
                            dve.wait_ge(hg_k, 8 + 1)
                        else:
                            dst = ev[:, u % 2, :]
                            if U_ZF + 2 <= u < U_HQ:
                                dve.wait_ge(z_sig, u - U_ZF - 1)
                            if U_HI + 2 <= u < U_DQ:
                                dve.wait_ge(tok_tr, u - U_HI - 1)
                            if U_DV <= u < U_HG:
                                dve.wait_ge(tok_tr, u - U_DV + 3)
                        if u == 0:
                            dve.wait_ge(rms_ready, 1)
                        dve.tensor_tensor(dst, unit_bank(u)[:], rms[:], ALU.mult).then_inc(unit_ev, 1)

                    def rope(n):
                        dve.wait_ge(unit_ev, U_DQ + n + 1)
                        dve.wait_ge(tables, 1)
                        t, q = tmp[:, n % 2, :], QK[:, n, :]
                        ch(dve.scalar_tensor_tensor(t, q, R[:, R_QG + n // 4:R_QG + n // 4 + 1], cosT, ALU.mult, ALU.mult))
                        dve.wait_ge(qk_aux, n + 1)
                        dve.tensor_tensor(q, bank[7][:], sinT, ALU.mult).then_inc(rope_cr, 1)
                        dve.wait_ge(rope_cr, n + 1)
                        ch(dve.tensor_tensor(q, q, t, ALU.add))
                        dve.wait_ge(qk_rstd, n + 1)
                        dve.tensor_tensor(q, q, rstd[:, n % 2, :], ALU.mult).then_inc(rope_done, 1)

                    def forget(n):
                        d, hd = divmod(n, 4)
                        dve.wait_ge(z_sig, n + 1)
                        if n:
                            dve.wait_ge(z_done, n)
                        s_p, s_n, f = sp[:, n % 2, :], sn[:, n % 2, :], head(T, d, hd)
                        ch(dve.tensor_scalar(tt, s_p, e30, 1.0, ALU.mult, ALU.min))
                        ch(dve.tensor_tensor(tt, tt, s_n, ALU.mult))
                        ch(dve.scalar_tensor_tensor(f, tt, lb[:, n:n + 1], s_p, ALU.mult, ALU.add))
                        ch(dve.tensor_scalar(f, f, 1.0, None, ALU.min))
                        dve.tensor_scalar(head(KK, d, hd), s_n, omlb[:, n:n + 1], None, ALU.mult).then_inc(z_done, 1)

                    def prep(pair):
                        cols = slice(pair * 2 * S, (pair + 1) * 2 * S)
                        if pair:
                            dve.wait_ge(lv_mm, 2 * 7 + 2)
                        dve.wait_ge(z_done, 8)
                        ch(dve.tensor_tensor(kx[:].rearrange("p a t -> p (a t)"), KK[:, 0, cols], KK[:, 1, cols], ALU.add))
                        dve.wait_ge(unit_ev, U_HQ + 2 * pair + 2)
                        dve.tensor_tensor(QQ[:, 0, cols], QQ[:, 1, cols], T[:, 1, cols], ALU.mult).then_inc(hg_q, 1)

                    def item(n):
                        pair, lv = divmod(n, LEVELS + 1)
                        cols = slice(pair * 2 * S, (pair + 1) * 2 * S)
                        if lv == 0:
                            dve.wait_ge(hg_q, 10 * pair + 1)
                            dve.wait_ge(lv_mm, 22 * pair + 2)
                            dve.tensor_tensor(QQ[:, 1, cols], QQ[:, 1, cols], T[:, 0, cols], ALU.mult).then_inc(hg_q, 1)
                        if n == 1:
                            dve.wait_ge(masks_in, 16)
                        if 1 <= lv <= 7:
                            m = M[:, (lv - 1) * P:lv * P].rearrange("p (o t) -> p o t", o=1).to_broadcast([P, TT, P])
                            for r in range(2):
                                dve.wait_ge(lv_mm, 22 * pair + 2 * lv + r + 1)
                                if lv == 1:
                                    dve.wait_ge(a_cp, 8 * pair + r + 1)
                                else:
                                    dve.wait_ge(a_msk, 14 * pair + 2 * (lv - 2) + r + 1)
                                dve.copy_predicated(diag(r), m, bank[2 + r][:].rearrange("p (i t) -> p i t", i=TT))\
                                   .then_inc(a_msk, 1)
                        if 1 <= lv <= 8:
                            h = 2 ** (lv - 1)
                            dve.wait_ge(lv_mm, 22 * pair + 2 * lv + 2)
                            dve.wait_ge(hg_q, 10 * pair + lv + 1)
                            if lv > 1:
                                dve.wait_ge(tot_ready, 7 * pair + lv - 1)
                            for half in range(2):
                                v = blocks(QQ[:, half, cols], h)[:, :, half, :]
                                w = totals(pair, h)[:, 1 - half, :].rearrange("p (n two o) -> p n two o", two=2, o=1)
                                last = dve.tensor_tensor(v, v, w[:, :, 1 - half, :].to_broadcast([P, S // h, h]), ALU.mult)
                            last.then_inc(hg_q, 1)
                        if lv == 1:
                            if pair:
                                dve.wait_ge(hg_k, 8)
                            for d in range(2):
                                w = totals(pair, 1)[:, d, :].rearrange("p (n two) -> p n two", two=2)
                                nxt = dve.tensor_tensor(totals(pair, 2)[:, d, :], w[:, :, 0], w[:, :, 1], ALU.mult)
                            nxt.then_inc(tot_ready, 1)

                    def row_max(a):
                        dve.wait_ge(sc_mm, a + 1)
                        for c in range(2):
                            m = dve.tensor_reduce(sm[:, a, c:c + 1], score_bank(a, c)[:], axis=AX.X, op=ALU.max, negate=True)
                        m.then_inc(neg_max, 1)

                    def combine(a):
                        dve.wait_ge(exps, a + 1)
                        ch(dve.reciprocal(sm[:, a, 4:6], sm[:, a, 2:4]))
                        ch(dve.tensor_tensor(sm[:, a, 6:7], sm[:, a, 5:6], lamc[:, 7:8], ALU.mult))
                        ch(dve.tensor_scalar(E[:, 0, :], E[:, 0, :], sm[:, a, 4:5], None, ALU.mult))
                        if a:
                            dve.wait_ge(tr_mm, a)
                        dve.scalar_tensor_tensor(W[:], E[:, 1, :], sm[:, a, 6:7], E[:, 0, :], ALU.mult, ALU.add)\
                           .then_inc(w_ready, 1)

                    def post(p):
                        kind, hd = HEAD_ORDER[p]
                        dve.wait_ge(o_rstd, p + 1)
                        if p >= 2:
                            dve.wait_ge(yL_ready, p - 1)
                        t = tmp[:, p % 2, :]
                        if kind == "hg":
                            ch(dve.scalar_tensor_tensor(t, out_head(p), R[:, R_HGG:R_HGG + 1], rstd[:, p % 2, :],
                                                        ALU.mult, ALU.mult))
                            dve.wait_ge(gs_done, hd + 1)
                            dve.tensor_tensor(t, t, gs(hd), ALU.mult).then_inc(y_ready, 1)
                        else:
                            dve.scalar_tensor_tensor(t, out_head(p), dag[:, 0:1], rstd[:, p % 2, :],
                                                     ALU.mult, ALU.mult).then_inc(y_ready, 1)

                    for kind, n in ORDER:
                        if kind == "unit":
                            evict(n)
                            if U_ZF < n <= U_HQ:
                                forget(n - U_ZF - 1)
                            if n == U_HQ + 1:
                                rotary(0)
                            if n == U_HI:
                                rotary(2)
                            if U_DQ < n <= U_DV:
                                rope(n - 1 - U_DQ)
                            if n == U_HG - 1:
                                row_max(0)
                        elif kind == "prep":
                            prep(n)
                            if n == 0:
                                rotary(1)
                        elif kind == "item":
                            item(n)
                        elif kind == "step":
                            combine(n)
                            for a in scores_after(n):
                                row_max(a)
                        elif kind == "post":
                            post(n)

                    for m_ in range(KT):
                        if m_ < KT - 1:
                            dve.wait_ge(wo_done, m_ + 1)
                        else:
                            dve.wait_ge(w_used, U_UP)
                        dve.tensor_tensor(x[:, m_, :], x[:, m_, :], bank[m_][:], ALU.add).then_inc(x_upd, 1)
                        if m_ >= 1:
                            low(dve, m_ - 1, 1, R_FFNG)
                    low(dve, KT - 1, 1, R_FFNG)
                    for q in range(2):
                        ch(dve.tensor_copy(cw[:, q, :], R[:, R_CONV + 8 * q:R_CONV + 8 * q + 8]))
                    dve.wait_ge(rms_ready, 2)

                    def pair(i, q, first, own):
                        for c in range(2):
                            dve.wait_ge(w_used, i * 4 + (U_UP + 2 * q + c + 1))
                            dve.tensor_tensor(uu[:, q, c, :], bank[2 * q + c][:], rms[:], ALU.mult).then_inc(up_ev, 1)
                        for c, dst in enumerate((ua, uv)):
                            w = lambda n: cw[:, q, 4 * c + n:4 * c + n + 1]
                            dve.wait_ge(conv_init, i * 4 + (2 * q + c + 1))
                            own(dve.scalar_tensor_tensor(dst[:, q, 1:S], uu[:, q, c, 0:S - 1], w(0), dst[:, q, 1:S],
                                                         ALU.mult, ALU.add))
                            dve.scalar_tensor_tensor(dst[:, q, 0:S - 1], uu[:, q, c, 1:S], w(2), dst[:, q, 0:S - 1],
                                                     ALU.mult, ALU.add).then_inc(conv_done, 1)
                        dve.wait_ge(silu_done, i * 2 + (q + 1))
                        dve.wait_ge(conv_done, i * 4 + (2 * q + 2))
                        dve.tensor_tensor(gt[:, q, :], ua[:, q, :], uv[:, q, :], ALU.mult).then_inc(g_ready, 1)
                        dve.wait_ge(gH_ready, i * 2 + (q + 1))
                        at = slice(q * S, q * S + S) if first else bass.ds(i * (2 * S) + q * S, S)
                        dve.tensor_tensor(gL[:, at], gt[:, q, :], gH[:, at].bitcast(F32), ALU.subtract)\
                           .then_inc(gL_ready, 1)
                        dve.wait_ge(gL_ready, i * 2 + (q + 1))
                        at = R_CONV + 8 * (q + 2)
                        nxt = R[:, at:at + 8] if first else R[:, bass.ds(i * 16 + at, 8)]
                        own(dve.tensor_copy(cw[:, q, :], nxt))

                    own = Chain(dve, dve_ffn)
                    for q in range(2):
                        pair(0, q, True, own)
                    per = own.n
                    with dve.Fori(1, FT // 2) as i:
                        own = Chain(dve, dve_ffn, i * per)
                        for q in range(2):
                            pair(i, q, False, own)
                    for m_ in range(KT):
                        if m_ < KT - 1:
                            dve.wait_ge(wd_done, m_ + 1)
                        else:
                            dve.wait_ge(w_used, UNITS)
                        dve.tensor_tensor(x[:, m_, :], x[:, m_, :], bank[m_][:], ALU.add).then_inc(x_upd, 1)
                        if m_ in (4, 6):
                            low(dve, m_ // 2 - 2, 2, R_MIXG)

            with nc.Block() as block:
                start = {par_in: 16, raw_in[0]: 16, raw_in[1]: 16, w_high: 1, w_split: 1,
                         hH_ready: LEAD_HIGH, hL_ready: LEAD_LOW}

                def restart(eng, share):
                    for s in layer_sems[share::5]:
                        eng.sem_clear(s)
                        if s in start:
                            eng.sem_inc(s, start[s])

                @block.sync
                def _(sp_):
                    restart(sp_, 0)

                @block.scalar
                def _(act):
                    restart(act, 1)

                @block.vector
                def _(dve):
                    restart(dve, 2)

                @block.gpsimd
                def _(pool):
                    restart(pool, 3)

                @block.tensor
                def _(pe):
                    restart(pe, 4)

        with nc.Block() as block:
            @block.sync
            def _(sp_):
                sp_.wait_ge(out_done, 16 * KT)


def constants():
    c = np.zeros((P, NC), np.float32)
    i = np.arange(P)
    c[:, C_IDENT:C_IDENT + P] = np.eye(P)
    c[:, C_MEAN_D:C_MEAN_D + P] = 1 / D
    c[:, C_MEAN_H:C_MEAN_H + P] = (i[:, None] // HD == i[None, :] // HD) / HD
    half = HD // 2
    for m in range(P):
        if m % HD < half:
            c[m + half, C_ROT + m] = -1
        else:
            c[m - half, C_ROT + m] = 1
    freq = np.float32(10000.0) ** (-np.arange(half, dtype=np.float32) / np.float32(half))
    c[:, C_FREQ] = freq[i % half]
    for l in range(DEPTH):
        lam_init = 0.8 - 0.6 * float(np.exp(-0.3 * l))
        c[:, C_LAM + l] = lam_init
        c[:, C_OML + l] = 1 - lam_init
    c[:, C_EPS] = EPS
    c[:, C_LN8] = -0.5 * np.log(HD)
    return c


def masks():
    i = np.arange(P)
    return np.concatenate([((i[:, None] // h) ^ 1) == i[None, :] // h for h in 2 ** np.arange(7)], axis=1)\
        .astype(np.uint8).view(np.int32)


def columns(w):
    d, r, n = w.shape
    return w.reshape(d, KT, P, n // P, P).transpose(0, 3, 2, 1, 4).reshape(d, n // P, P, KT * P)


def kernel(**inputs):
    import concourse.bacc as bacc
    from concourse.bass_utils import run_bass_kernel_spmd

    g = {k: np.asarray(v) for k, v in inputs.items()}
    w_in = g["w_in"]
    part = [w_in[:, :, n * 512:(n + 1) * 512] for n in range(8)]
    w_up = columns(g["w_up"]).reshape(DEPTH, 2, FT, P, UNIT).transpose(0, 2, 1, 3, 4).reshape(DEPTH, 2 * FT, P, UNIT)
    w_out = g["w_out"].reshape(DEPTH, KT, P, UNIT)[:, [hd + (4 if kind == "hg" else 0) for kind, hd in HEAD_ORDER]]
    w_down = g["w_down"].reshape(DEPTH, FT, P, UNIT)
    wts = np.concatenate([columns(part[n]) for n in (4, 5, 3, 6, 0, 1, 2, 7)] + [w_out, w_up, w_down],
                         axis=1).reshape(DEPTH * UNITS, P, UNIT)
    wts = np.concatenate([wts, np.zeros((2, P, UNIT), np.float32)])
    par = np.zeros((DEPTH + 1, P, NR), np.float32)
    par[:DEPTH, :, R_MIXG:R_MIXG + 8] = g["mix_norm_g"].reshape(DEPTH, KT, P).transpose(0, 2, 1)
    par[:DEPTH, :, R_FFNG:R_FFNG + 8] = g["ffn_norm_g"].reshape(DEPTH, KT, P).transpose(0, 2, 1)
    for col, name in ((R_QG, "q_norm_g"), (R_KG, "k_norm_g"), (R_LAM, "lam_q1"), (R_LAM + 1, "lam_k1"),
                      (R_LAM + 2, "lam_q2"), (R_LAM + 3, "lam_k2")):
        par[:DEPTH, :, col] = np.concatenate([g[name], g[name]], axis=1)
    par[:DEPTH, :, R_DAG] = g["diff_out_g"]
    par[:DEPTH, :, R_HGG] = g["hg_out_g"]
    conv = np.concatenate([g["conv_w"], g["conv_b"][:, None]], axis=1)
    conv = conv.reshape(DEPTH, 4, 2, FT, P).transpose(0, 4, 3, 2, 1)
    par[:DEPTH, :, R_CONV:R_CONV + 8 * FT] = conv.reshape(DEPTH, P, 8 * FT)
    lbl = np.ascontiguousarray(g["hg_lb_logits"].reshape(DEPTH, 8, P).transpose(2, 0, 1))
    pos = np.ascontiguousarray(np.broadcast_to(g["positions"].reshape(1, S), (P, S)))
    xT = np.ascontiguousarray(g["x"].reshape(S, KT, P).transpose(2, 1, 0))
    arrays = {"xT": xT, "wts": wts, "cst": constants(), "msk": masks(), "par": par, "lbl": lbl, "pos": pos}

    nc = bacc.Bacc("TRN2", target_bir_lowering=False, num_devices=1)
    aps = {k: nc.dram_tensor(k, a.shape, mybir.dt.from_np(a.dtype), kind="ExternalInput").ap() for k, a in arrays.items()}
    out = nc.dram_tensor("outT", (P, KT, S), F32, kind="ExternalOutput").ap()
    build(nc, *[aps[k] for k in ("xT", "wts", "cst", "msk", "par", "lbl", "pos")], out)
    r = run_bass_kernel_spmd(nc, [arrays], core_ids=[0])
    y = np.asarray(r.results[0]["outT"])
    return np.ascontiguousarray(y.transpose(2, 1, 0)).reshape(1, S, D)
```
